# Optimizing a Trainium2 kernel written in Bass

```python
import jax, jax.numpy as jnp
from jax import lax
import numpy as np

D_MODEL = 1024
BATCH = 1
SEQ = 256
DEPTH = 2

HEAD_DIM = 64
N_Q_HEADS = 8
N_KV_HEADS = 2
GQA_GROUP = N_Q_HEADS // N_KV_HEADS
ATTN_WIDTH = N_Q_HEADS * HEAD_DIM
KV_WIDTH = N_KV_HEADS * HEAD_DIM
WINDOW = 128
BLOCK = 128
CONV_WIDTH = D_MODEL - ATTN_WIDTH
CONV_KERNEL = 31
IN_PROJ_WIDTH = ATTN_WIDTH + 2 * KV_WIDTH + 2 * CONV_WIDTH
D_FF_DENSE = 2816
N_EXPERTS = 8
TOP_K = 2
D_FF_EXPERT = 3584
N_DENSE = (DEPTH + 1) // 2
N_MOE = DEPTH // 2
NORM_EPS = 1e-6

kernel_name = "hybrid_swa_sink_conformer_moe"

def rms_norm(x, g):
    xf = x.astype(jnp.float32)
    y = xf * lax.rsqrt(jnp.mean(xf * xf, axis=-1, keepdims=True) + NORM_EPS)
    return (y * g.astype(jnp.float32)).astype(x.dtype)

def layer_norm(x, g, b):
    xf = x.astype(jnp.float32)
    mu = jnp.mean(xf, axis=-1, keepdims=True)
    var = jnp.mean(jnp.square(xf - mu), axis=-1, keepdims=True)
    y = (xf - mu) * lax.rsqrt(var + NORM_EPS)
    return (y * g.astype(jnp.float32) + b.astype(jnp.float32)).astype(x.dtype)

def alibi_slopes():
    h = jnp.arange(1, N_Q_HEADS + 1, dtype=jnp.float32)
    return jnp.exp2(-8.0 * h / N_Q_HEADS)

def sliding_window_attention(q, k, v, sinks):
    B, S = q.shape[0], q.shape[1]
    nb = S // BLOCK
    qb = q.reshape(B, nb, BLOCK, N_KV_HEADS, GQA_GROUP, HEAD_DIM)

    def band(t):
        t = t.reshape(B, nb, BLOCK, N_KV_HEADS, HEAD_DIM)
        prev = jnp.pad(t, ((0, 0), (1, 0), (0, 0), (0, 0), (0, 0)))[:, :-1]
        return jnp.concatenate([prev, t], axis=2)

    kb, vb = band(k), band(v)
    scores = jnp.einsum('bnqkgd,bnskd->bnkgqs', qb, kb,
                        preferred_element_type=jnp.float32) * (HEAD_DIM ** -0.5)
    dist = (jnp.arange(BLOCK)[:, None] + BLOCK) - jnp.arange(2 * BLOCK)[None, :]
    valid = (dist >= 0) & (dist < WINDOW)
    first_blk_pad = (jnp.arange(nb)[:, None, None] == 0) & (jnp.arange(2 * BLOCK) < BLOCK)[None, None, :]
    valid = valid[None] & ~first_blk_pad
    slopes = alibi_slopes().reshape(N_KV_HEADS, GQA_GROUP)
    scores = scores - slopes[:, :, None, None] * dist.astype(jnp.float32)
    scores = jnp.where(valid[None, :, None, None], scores, -jnp.inf)
    sink = jnp.broadcast_to(sinks.astype(jnp.float32).reshape(N_KV_HEADS, GQA_GROUP, 1, 1),
                            scores.shape[:-1] + (1,))
    probs = jax.nn.softmax(jnp.concatenate([scores, sink], axis=-1), axis=-1)[..., :-1]
    out = jnp.einsum('bnkgqs,bnskd->bnqkgd', probs.astype(v.dtype), vb)
    return out.reshape(B, S, ATTN_WIDTH)

def conformer_conv(u, gate, w_dw, b_dw, ln_g, ln_b):
    h = u * jax.nn.sigmoid(gate)
    hp = jnp.pad(h, ((0, 0), (CONV_KERNEL - 1, 0), (0, 0)))
    h = lax.conv_general_dilated(hp, w_dw[:, None, :].astype(h.dtype), window_strides=(1,),
                                 padding='VALID', dimension_numbers=('NWC', 'WIO', 'NWC'),
                                 feature_group_count=CONV_WIDTH) + b_dw
    h = layer_norm(h, ln_g, ln_b)
    return jax.nn.silu(h)

def dense_swiglu(h, w_gate, w_up, w_down):
    return (jax.nn.silu(h @ w_gate) * (h @ w_up)) @ w_down

def moe_swiglu(h, w_router, w_gate, w_up, w_down):
    B, S, D = h.shape
    t = h.reshape(-1, D)
    logits = (t @ w_router).astype(jnp.float32)
    top_v, top_i = lax.top_k(logits, TOP_K)
    top_w = jax.nn.softmax(top_v, axis=-1)
    combine = jnp.sum(jax.nn.one_hot(top_i, N_EXPERTS, dtype=jnp.float32) * top_w[..., None], axis=1)
    out = jnp.zeros_like(t)
    for e in range(N_EXPERTS):
        y = (jax.nn.silu(t @ w_gate[e]) * (t @ w_up[e])) @ w_down[e]
        out = out + combine[:, e:e + 1].astype(t.dtype) * y
    return out.reshape(B, S, D)

def setup_inputs(seed: int = 0) -> dict:
    key = jax.random.key(seed)
    ks = jax.random.split(key, 24)
    f32 = jnp.float32
    nrm = lambda k, shape, scale: jax.random.normal(k, shape, f32) * scale
    return {
        "x": nrm(ks[0], (BATCH, SEQ, D_MODEL), 1.0),
        "attn_norm_g": 1.0 + nrm(ks[1], (DEPTH, D_MODEL), 0.02),
        "w_in": nrm(ks[2], (DEPTH, D_MODEL, IN_PROJ_WIDTH), D_MODEL ** -0.5),
        "q_norm_g": 1.0 + nrm(ks[3], (DEPTH, HEAD_DIM), 0.02),
        "k_norm_g": 1.0 + nrm(ks[4], (DEPTH, HEAD_DIM), 0.02),
        "sinks": nrm(ks[5], (DEPTH, N_Q_HEADS), 0.5),
        "conv_w": nrm(ks[6], (DEPTH, CONV_KERNEL, CONV_WIDTH), CONV_KERNEL ** -0.5),
        "conv_b": nrm(ks[7], (DEPTH, CONV_WIDTH), 0.02),
        "conv_ln_g": 1.0 + nrm(ks[8], (DEPTH, CONV_WIDTH), 0.02),
        "conv_ln_b": nrm(ks[9], (DEPTH, CONV_WIDTH), 0.02),
        "w_out": nrm(ks[10], (DEPTH, D_MODEL, D_MODEL), D_MODEL ** -0.5),
        "ffn_norm_g": 1.0 + nrm(ks[11], (DEPTH, D_MODEL), 0.02),
        "dense_w_gate": nrm(ks[12], (N_DENSE, D_MODEL, D_FF_DENSE), D_MODEL ** -0.5),
        "dense_w_up": nrm(ks[13], (N_DENSE, D_MODEL, D_FF_DENSE), D_MODEL ** -0.5),
        "dense_w_down": nrm(ks[14], (N_DENSE, D_FF_DENSE, D_MODEL), D_FF_DENSE ** -0.5),
        "w_router": nrm(ks[15], (N_MOE, D_MODEL, N_EXPERTS), D_MODEL ** -0.5),
        "moe_w_gate": nrm(ks[16], (N_MOE, N_EXPERTS, D_MODEL, D_FF_EXPERT), D_MODEL ** -0.5),
        "moe_w_up": nrm(ks[17], (N_MOE, N_EXPERTS, D_MODEL, D_FF_EXPERT), D_MODEL ** -0.5),
        "moe_w_down": nrm(ks[18], (N_MOE, N_EXPERTS, D_FF_EXPERT, D_MODEL), D_FF_EXPERT ** -0.5),
    }

def reference(x, attn_norm_g, w_in, q_norm_g, k_norm_g, sinks, conv_w, conv_b, conv_ln_g,
              conv_ln_b, w_out, ffn_norm_g, dense_w_gate, dense_w_up, dense_w_down,
              w_router, moe_w_gate, moe_w_up, moe_w_down):
    B, S, _ = x.shape
    o_k = ATTN_WIDTH
    o_v = o_k + KV_WIDTH
    o_c = o_v + KV_WIDTH
    o_g = o_c + CONV_WIDTH
    for layer in range(DEPTH):
        h = rms_norm(x, attn_norm_g[layer])
        proj = h @ w_in[layer]
        q = proj[..., :o_k].reshape(B, S, N_Q_HEADS, HEAD_DIM)
        k = proj[..., o_k:o_v].reshape(B, S, N_KV_HEADS, HEAD_DIM)
        v = proj[..., o_v:o_c].reshape(B, S, N_KV_HEADS, HEAD_DIM)
        q = rms_norm(q, q_norm_g[layer])
        k = rms_norm(k, k_norm_g[layer])
        attn_out = sliding_window_attention(q, k, v, sinks[layer])
        conv_out = conformer_conv(proj[..., o_c:o_g], proj[..., o_g:], conv_w[layer],
                                  conv_b[layer], conv_ln_g[layer], conv_ln_b[layer])
        x = x + jnp.concatenate([attn_out, conv_out], axis=-1) @ w_out[layer]
        h = rms_norm(x, ffn_norm_g[layer])
        if layer % 2 == 0:
            i = layer // 2
            x = x + dense_swiglu(h, dense_w_gate[i], dense_w_up[i], dense_w_down[i])
        else:
            i = layer // 2
            x = x + moe_swiglu(h, w_router[i], moe_w_gate[i], moe_w_up[i], moe_w_down[i])
    return x


_drawn_inputs = setup_inputs


def setup_inputs(seed=0):
    import zlib

    import numpy as np

    out = dict(_drawn_inputs(seed))
    spreads = {}
    factors = {'q_norm_g': 3.058, 'k_norm_g': 5.324, 'sinks': 2.879}
    for name, (base, spread) in spreads.items():
        noise = np.random.default_rng([zlib.crc32(name.encode()), seed]).standard_normal(out[name].shape)
        drawn = base * np.exp(spread * noise) if base else spread * noise
        out[name] = __import__('jax').numpy.asarray(drawn.astype(out[name].dtype))
    for name, factor in factors.items():
        out[name] = (out[name] * factor).astype(out[name].dtype)
    return out
```

```python
from contextlib import ExitStack

import concourse.bass as bass
from concourse import mybir

F32 = mybir.dt.float32
F32R = mybir.dt.float32r
I32 = mybir.dt.int32
ALU = mybir.AluOpType
ACT = mybir.ActivationFunctionType
AX = mybir.AxisListType

P = 128
WINDOW = 128
RAW_RING = 6
PART_RING = 3
SLOT = 2048
TERMS = ((0, 0), (0, 1), (1, 0))


def hybrid_trunk(nc, x, attn_norm_g, w_in, q_norm_g, k_norm_g, sinks, conv_w, conv_b, conv_ln_g,
                 conv_ln_b, w_out, ffn_norm_g, dense_w_gate, dense_w_up, dense_w_down,
                 w_router, moe_w_gate, moe_w_up, moe_w_down, out):
    _, S, D = x.shape
    L, _, IN_W = w_in.shape
    HD = q_norm_g.shape[1]
    NH = sinks.shape[1]
    TAPS, CW = conv_w.shape[1], conv_w.shape[2]
    AW = NH * HD
    KVW = (IN_W - AW - 2 * CW) // 2
    NKV = KVW // HD
    DFF = dense_w_gate.shape[2]
    NE, EFF = moe_w_gate.shape[1], moe_w_gate.shape[3]
    NB = S // P
    KC = D // P
    CC = CW // P
    HP = NH // 2
    PAD = TAPS - 1
    EPS = 1e-6
    NPRM = TAPS + 3
    assert NB == 2 and KC == 8 and CC == 4 and HD == 64 and NKV == 2 and NH == 8 and L == 2

    FRONT_SLOTS = 11
    DG = DFF // 256
    EG = EFF // 512
    S_FRONT = [0, FRONT_SLOTS + 3 * DG]
    S_DENSE = FRONT_SLOTS
    S_MOE = S_FRONT[1] + FRONT_SLOTS
    PAIR = 6 * 2 * EG
    S_OVER = S_MOE + NE * EG * 6
    OVER = 6 * EG

    def at(i, per, const):
        return const if i is None else i * per + const

    with ExitStack() as ctx:
        def sb(name, shape, dt=F32):
            return ctx.enter_context(nc.sbuf_tensor(name, shape, dt))

        def sem(name):
            return ctx.enter_context(nc.semaphore(name))

        raw = sb("raw", [P, RAW_RING, SLOT])
        w_part = [sb("w_high", [P, PART_RING, SLOT], F32R), sb("w_low", [P, PART_RING, SLOT], F32R)]
        xr = sb("xr", [P, NB, D])
        h_td = sb("h_td", [P, NB, D])
        hT = [sb("hT_high", [P, KC, S], F32R), sb("hT_low", [P, KC, S], F32R)]
        cat = [sb("cat_high", [P, KC, S], F32R), sb("cat_low", [P, KC, S], F32R)]
        act_part = [sb("act_high", [P, 2, 512], F32R), sb("act_low", [P, 2, 512], F32R)]
        gnorm = sb("gnorm", [P, 2, D])
        hpad = sb("hpad", [P, CC, PAD + S])
        cacc = sb("cacc", [P, CC, S])
        v_sb = sb("v_sb", [P, NB, KVW])
        sc0 = sb("sc0", [P, NH, P + 1])
        work_a = sb("work_a", [P, 3072])
        work_b = sb("work_b", [P, NH * (2 * P + 1)])
        ctmp = sb("ctmp", [P, 2, S])
        ndist = sb("ndist", [P, 2 * P])
        ident = sb("ident", [P, P])
        ones = sb("ones", [P, P])
        mean_w = sb("mean_w", [P, P])
        tri = sb("tri", [P, P])
        pcol = sb("pcol", [P, L, CC, NPRM])
        qkg = sb("qkg", [P, L, 2, HD])
        sink_b = sb("sink_b", [P, L, NH])
        eps_t = sb("eps_t", [P, 1])
        ss = sb("ss", [P, 4, NB])
        rms = sb("rms", [P, 4, NB])
        rstd = sb("rstd", [P, 4, NB])
        qkss = sb("qkss", [P, NB * (NH + NKV)])
        qkr = sb("qkr", [P, NB * (NH + NKV)])
        mx = sb("mx", [P, NB, NH])
        psums = sb("psums", [P, NB, NH])
        pinv = sb("pinv", [P, NB, NH])
        wr = sb("wr", [P, KC, NE])
        iota_c = sb("iota_c", [P, P])
        base_e = sb("base_e", [P, NE])
        base_ei = sb("base_ei", [P, NE], I32)
        tri8 = sb("tri8", [P, NE, NE])
        lg = sb("lg", [P, NB, NE])
        cmp_a = sb("cmp_a", [P, NB, NE, NE])
        cmp_b = sb("cmp_b", [P, NB, NE, NE])
        rank = sb("rank", [P, NB, NE])
        selr = sb("selr", [P, 2, NB, NE])
        sel = sb("sel", [P, NB, NE])
        possel = sb("possel", [P, NB, NE])
        pos = sb("pos", [P, NB, NE])
        tmp8 = sb("tmp8", [P, 2, NB, NE])
        top_l = sb("top_l", [P, 2, NB])
        top_w = sb("top_w", [P, 2, NB])
        zt = sb("zt", [P, NB])
        den = sb("den", [P, NB])
        row_d = sb("row_d", [P, NE])
        row_f = sb("row_f", [P, 2, NB])
        row_i = sb("row_i", [P, 2, NB], I32)
        over_f = sb("over_f", [P, NE])
        over_i = sb("over_i", [P, NE], I32)
        before_i = sb("before_i", [P, NE + 1], I32)
        before_f = sb("before_f", [P, NE + 1])
        ps = ctx.enter_context(nc.psum_tensor("ps", [P, 8, 512], F32))
        MAX_OVER = (2 * S) // (P + 1)
        y_dram = nc.dram_tensor("y_slots", ((NE + MAX_OVER) * P, D), F32, kind="Internal").ap()

        zero_r = sb("zero_r", [P, P], F32R)
        CONST_LOADS = 16 * 11
        DVE_CONSTS = 5
        GATHER_AT = 3

        h_flat = h_td[:, :, :].rearrange("p b d -> p (b d)")
        sig = h_flat[:, 0:CC * S].rearrange("p (c t) -> p c t", c=CC)
        q_n = h_flat[:, 0:NB * AW].rearrange("p (b n) -> p b n", b=NB)
        q_sq = h_flat[:, D:D + NB * AW].rearrange("p (b n) -> p b n", b=NB)
        ln_sq = sig
        ln_sd = h_flat[:, D:D + S]
        ln_r = h_flat[:, D + S:D + 2 * S]
        k_sq = work_a[:, 0:NB * KVW].rearrange("p (b n) -> p b n", b=NB)
        k_n = work_a[:, NB * KVW:2 * NB * KVW].rearrange("p (b n) -> p b n", b=NB)
        kdup = work_a[:, 512:1024].rearrange("p (b g r d) -> p b g r d", b=NB, g=NKV, r=2)
        kT = work_a[:, 1024:1536].rearrange("p (g t) -> p g t", g=NKV)
        qT = work_a[:, 2048:3072].rearrange("p (j t) -> p j t", j=HP)
        prm = work_b[0:NPRM, 0:L * CW].rearrange("n (l c) -> n l c", l=L)
        pT = work_a[:, :].rearrange("p (m h q) -> p m h q", m=3, h=NH)
        sc1 = work_b[:, :].rearrange("p (h s) -> p h s", h=NH)
        scores = [sc0[:, :, :], sc1]
        onehot = work_b[:, 0:NB * NE * P].rearrange("p (b e c) -> p b e c", b=NB, e=NE)
        hT_plain = work_a[:, 0:KC * S].rearrange("p (k t) -> p k t", k=KC)
        y_sb = work_a[:, 0:D]
        silu_t = work_a[:, 2048:2560]
        prod_t = work_a[:, 2560:3072]
        xg = [t[:, :, :].rearrange("p k (r c) -> p k r c", r=2) for t in hT]
        y_rows = raw[:, 0:4, 0:D]

        x_loaded = sem("x_loaded")
        consts_loaded = sem("consts_loaded")
        gain_loaded = [sem("gain_loaded0"), sem("gain_loaded1")]
        landed = [sem(f"landed{i}") for i in range(RAW_RING)]
        slot_claimed = sem("slot_claimed")
        w_high_done = sem("w_high_done")
        w_low_done = sem("w_low_done")
        w_used = sem("w_used")
        pool_consts = sem("pool_consts")
        dve_consts = sem("dve_consts")
        prm_turned = sem("prm_turned")
        prm_ready = sem("prm_ready")
        sq_done = sem("sq_done")
        rms_done = sem("rms_done")
        rstd_done = sem("rstd_done")
        h_done = sem("h_done")
        h_turned = sem("h_turned")
        hT_high_done = sem("hT_high_done")
        hT_low_done = sem("hT_low_done")
        sig_done = sem("sig_done")
        glu_done = sem("glu_done")
        conv_dve = sem("conv_dve")
        conv_pool = sem("conv_pool")
        qk_sq_done = sem("qk_sq_done")
        v_done = sem("v_done")
        qk_ss_done = sem("qk_ss_done")
        qk_rms_done = sem("qk_rms_done")
        qk_step = sem("qk_step")
        qk_turned = sem("qk_turned")
        qkT_done = sem("qkT_done")
        scored = sem("scored")
        biased = sem("biased")
        max_done = sem("max_done")
        exp_done = sem("exp_done")
        probs_done = sem("probs_done")
        dve_step = sem("dve_step")
        qk_ready = sem("qk_ready")
        p_turned = sem("p_turned")
        pT_done = sem("pT_done")
        pv_done = sem("pv_done")
        cat_high_done = sem("cat_high_done")
        cat_low_done = sem("cat_low_done")
        ln_sum = sem("ln_sum")
        ln_step = sem("ln_step")
        ln_sq_done = sem("ln_sq_done")
        ln_sd_done = sem("ln_sd_done")
        silu_c = sem("silu_c")
        x_added = sem("x_added")
        silu_done = sem("silu_done")
        prod_done = sem("prod_done")
        act_turned = sem("act_turned")
        act_high_done = sem("act_high_done")
        act_low_done = sem("act_low_done")
        hT_plain_done = sem("hT_plain_done")
        routed = sem("routed")
        sel_done = sem("sel_done")
        shifted = sem("shifted")
        zdiff_done = sem("zdiff_done")
        onehot_done = sem("onehot_done")
        rows_ready = sem("rows_ready")
        over_ready = sem("over_ready")
        z_done = sem("z_done")
        counted = sem("counted")
        gathered = sem("gathered")
        xg_high_done = sem("xg_high_done")
        xg_low_done = sem("xg_low_done")
        y_copied = sem("y_copied")
        y_stored = sem("y_stored")
        y_free = sem("y_free")
        zeros_stored = sem("zeros_stored")
        passes_ended = sem("passes_ended")
        rows_fetched = [sem(f"rows_fetched{i}") for i in range(4)]
        combined = sem("combined")
        out_stored = sem("out_stored")

        w_in_v = w_in.rearrange("l (k p) n -> l p k n", p=P)
        w_out_v = w_out.rearrange("l (k p) n -> l p k n", p=P)
        dg_v = dense_w_gate.rearrange("o (k p) f -> (o p) k f", p=P)
        du_v = dense_w_up.rearrange("o (k p) f -> (o p) k f", p=P)
        dd_v = dense_w_down.rearrange("o (k p) n -> (o p) k n", p=P)
        eg_v = moe_w_gate.rearrange("o e (k p) f -> (o e) p k f", p=P)
        eu_v = moe_w_up.rearrange("o e (k p) f -> (o e) p k f", p=P)
        ed_v = moe_w_down.rearrange("o e (k p) n -> (o e) p k n", p=P)
        x_v = x.rearrange("o (b p) d -> p (o b) d", p=P)
        out_v = out.rearrange("o (b p) d -> p (o b) d", p=P)
        VAL, GATE = AW + 2 * KVW, AW + 2 * KVW + CW

        def passes_in_all(eng):
            eng.wait_ge(over_ready, 1)
            return eng.value_load(before_i[0:1, NE:NE + 1], min_val=0, max_val=MAX_OVER)

        def overflow_passes(eng, n_passes, one_pass):
            with eng.If(n_passes > 0):
                with eng.Fori(0, NE) as e:
                    over = eng.value_load(over_i[0:1, bass.ds(e, 1)], min_val=0, max_val=1)
                    with eng.If(over > 0):
                        m = eng.value_load(before_i[0:1, bass.ds(e, 1)], min_val=0, max_val=MAX_OVER - 1)
                        one_pass(e, m)
                eng.sem_inc(passes_ended, 1)

        def head_place(h):
            return h % 2 * (NH // 2) + h // 2

        def raw_slot(s, k):
            return raw[:, s % RAW_RING, :].rearrange("p (k n) -> p k n", k=k)

        def part_slot(part, s, k):
            return w_part[part][:, s % PART_RING, :].rearrange("p (k n) -> p k n", k=k)

        block = ctx.enter_context(nc.Block())

        @block.sync
        def _(sp):
            def load(s, src, k, i=None, per=0):
                if s >= RAW_RING:
                    sp.wait_ge(w_low_done, at(i, per, s - RAW_RING + 1))
                if i is not None:
                    sp.sem_inc(slot_claimed, 1)
                sp.dma_start(raw_slot(s, k), src).then_inc(landed[s % RAW_RING], 16)

            def front(l):
                b = S_FRONT[l]
                for n, col in enumerate((VAL, GATE, 0)):
                    for j in range(2):
                        load(b + 2 * n + j, w_in_v[l, :, 4 * j:4 * j + 4, col:col + 512], 4)
                load(b + 6, w_in_v[l, :, :, AW:AW + 2 * KVW], 8)
                for j in range(4):
                    load(b + 7 + j, w_out_v[l, :, 2 * j:2 * j + 2, :], 2)

            def dense_gate_up(s, col, i=None):
                load(s, dg_v[:, :, bass.ds(col, 256)], 8, i, 6)
                load(s + 1, du_v[:, :, bass.ds(col, 256)], 8, i, 6)

            def dense_down(s, row, i=None):
                load(s, dd_v[:, bass.ds(row, 2), :], 2, i, 6)

            def gate_up(s, e, g, i, per):
                for n, v in enumerate((eg_v, eu_v)):
                    for j in range(2):
                        load(s + 2 * n + j, v[e, :, 4 * j:4 * j + 4, 512 * g:512 * g + 512], 4, i, per)

            def down(s, e, g, i, per):
                for j in range(2):
                    load(s + j, ed_v[e, :, 4 * g + 2 * j:4 * g + 2 * j + 2, :], 2, i, per)

            def expert_steps(s, experts, following, i, per):
                groups = [(e, g) for e in experts for g in range(EG)]
                for n, (e, g) in enumerate(groups):
                    after = groups[n + 1] if n + 1 < len(groups) else following
                    if after is not None:
                        gate_up(s + 6 * n, *after, i, per)
                    down(s + 6 * n + (4 if after is not None else 0), e, g, i, per)

            sp.dma_start(xr[:, :, :], x_v).then_inc(x_loaded, 16)
            front(0)
            dense_gate_up(S_DENSE, 0)
            with sp.Fori(0, (DG - 1) // 2) as i:
                for u in range(2):
                    dense_gate_up(S_DENSE + 2 + 3 * u, i * 512 + 256 * (u + 1), i)
                    dense_down(S_DENSE + 4 + 3 * u, i * 4 + 2 * u, i)
            dense_down(S_DENSE + 3 * DG - 1, 2 * (DG - 1))
            front(1)
            gate_up(S_MOE, 0, 0, None, 0)

            def one_pass(e, m):
                gate_up(S_OVER, e, 0, m, OVER)
                expert_steps(S_OVER + 4, (e,), None, m, OVER)

            with sp.Fori(0, NE // 2 - 1) as i:
                expert_steps(S_MOE + 4, (i * 2, i * 2 + 1), (i * 2 + 2, 0), i, PAIR)
            expert_steps(S_MOE + 4 + (NE // 2 - 1) * PAIR, (NE - 2, NE - 1), None, None, 0)
            overflow_passes(sp, passes_in_all(sp), one_pass)
            sp.wait_ge(combined, 4)
            sp.dma_start(out_v, xr[:, :, :]).then_inc(out_stored, 16)
            sp.wait_ge(out_stored, 16)

        @block.gpsimd
        def _(pool):
            def bcast(ap):
                return ap.partition_broadcast(P)
            pool.sem_inc(y_free, 1)
            pool.dma_start(prm[0:TAPS, :, :], conv_w.rearrange("l k c -> k l c")).then_inc(consts_loaded, 16)
            for r, v in enumerate((conv_b, conv_ln_g, conv_ln_b)):
                pool.dma_start(prm[TAPS + r:TAPS + r + 1, :, :], v.rearrange("(o l) c -> o l c", o=1)).then_inc(consts_loaded, 16)
            pool.dma_start(gnorm[:, 0, :], bcast(attn_norm_g[0])).then_inc(gain_loaded[0], 16)
            pool.dma_start(gnorm[:, 1, :], bcast(ffn_norm_g[0])).then_inc(gain_loaded[1], 16)
            for l in range(L):
                pool.dma_start(qkg[:, l, 0, :], bcast(q_norm_g[l])).then_inc(consts_loaded, 16)
                pool.dma_start(qkg[:, l, 1, :], bcast(k_norm_g[l])).then_inc(consts_loaded, 16)
                pool.dma_start(sink_b[:, l, :], bcast(sinks[l])).then_inc(consts_loaded, 16)
            pool.dma_start(wr[:, :, :], w_router.rearrange("o (k p) e -> p (o k) e", p=P)).then_inc(consts_loaded, 16)
            pool.memset(ident[:, :], 0.0).then_inc(pool_consts, 1)
            pool.memset(tri[:, :], 1.0).then_inc(pool_consts, 1)
            pool.memset(tri8[:, :, :], 1.0).then_inc(pool_consts, 1)
            pool.iota(iota_c[:, :].bitcast(I32), pattern=[[1, P]], base=0, channel_multiplier=0).then_inc(pool_consts, 1)
            pool.iota(base_ei[:, :], pattern=[[P, NE]], base=0, channel_multiplier=0).then_inc(pool_consts, 1)
            pool.iota(ndist[:, :].bitcast(I32), pattern=[[1, 2 * P]], base=-P, channel_multiplier=-1).then_inc(pool_consts, 1)
            pool.wait_ge(pool_consts, 6)
            pool.affine_select(out=ident[:, :], in_=ident[:, :], compare_op=ALU.not_equal, fill=1.0, base=0,
                               pattern=[[-1, P]], channel_multiplier=1).then_inc(pool_consts, 1)
            pool.affine_select(out=tri[:, :], in_=tri[:, :], compare_op=ALU.is_ge, fill=0.0, base=-1,
                               pattern=[[1, P]], channel_multiplier=-1).then_inc(pool_consts, 1)
            pool.affine_select(out=tri8[:, :, :], in_=tri8[:, :, :], compare_op=ALU.is_ge, fill=0.0, base=-1,
                               pattern=[[1, NE], [-1, NE]], channel_multiplier=0).then_inc(pool_consts, 1)
            pool.tensor_copy(iota_c[:, :], iota_c[:, :].bitcast(I32)).then_inc(pool_consts, 1)
            pool.tensor_copy(base_e[:, :], base_ei[:, :]).then_inc(pool_consts, 1)
            pool.tensor_copy(ndist[:, :], ndist[:, :].bitcast(I32)).then_inc(pool_consts, 1)
            pool.wait_ge(pool_consts, 12)
            pool.affine_select(out=ndist[:, :], in_=ndist[:, :], compare_op=ALU.is_ge, fill=-1e30, base=P,
                               pattern=[[-1, 2 * P]], channel_multiplier=1).then_inc(pool_consts, 1)
            pool.wait_ge(pool_consts, 13)
            pool.affine_select(out=ndist[:, :], in_=ndist[:, :], compare_op=ALU.is_ge, fill=-1e30, base=WINDOW - 1 - P,
                               pattern=[[1, 2 * P]], channel_multiplier=-1).then_inc(pool_consts, 1)

            pool.memset(cacc[:, :, :], 0.0).then_inc(pool_consts, 1)
            pool.wait_ge(pool_consts, 15)
            for m in range(MAX_OVER):
                pool.dma_start(y_dram[(NE + m) * P:(NE + m + 1) * P, :], cacc[:, :, :].rearrange("p c t -> p (c t)")).then_inc(zeros_stored, 16)

            def conv(l):
                pool.wait_ge(glu_done, l + 1)
                pool.wait_ge(prm_ready, 1)
                c = CC - 1
                for tap in range(TAPS):
                    n = 2 * (TAPS * l + tap)
                    w = pcol[:, l, c, tap:tap + 1]
                    src = hpad[:, c, tap:tap + S]
                    if tap == 0:
                        pool.tensor_scalar(cacc[:, c, :], src, w, pcol[:, l, c, TAPS:TAPS + 1], ALU.mult, ALU.add).then_inc(conv_pool, 2)
                        continue
                    if tap > 2:
                        pool.wait_ge(conv_pool, n - 2)
                    pool.tensor_scalar(ctmp[:, tap % 2, :], src, w, None, ALU.mult).then_inc(conv_pool, 1)
                    pool.wait_ge(conv_pool, n + 1)
                    pool.tensor_tensor(cacc[:, c, :], cacc[:, c, :], ctmp[:, tap % 2, :], ALU.add).then_inc(conv_pool, 1)

            pool.wait_ge(zeros_stored, 16 * MAX_OVER)
            conv(0)
            pool.wait_ge(h_done, 2)
            pool.dma_start(gnorm[:, 0, :], bcast(attn_norm_g[1])).then_inc(gain_loaded[0], 16)
            pool.wait_ge(h_done, 4)
            pool.dma_start(gnorm[:, 1, :], bcast(ffn_norm_g[1])).then_inc(gain_loaded[1], 16)
            conv(1)
            n_passes = passes_in_all(pool)

            def store(m):
                pool.wait_ge(y_copied, m + 2)
                pool.dma_start(y_dram[bass.ds(m * P, P), :], y_sb).then_inc(y_stored, 16)
                pool.wait_ge(y_stored, (m + 1) * 16)
                pool.sem_inc(y_free, 1)

            with pool.Fori(0, NE) as e:
                store(e)
            overflow_passes(pool, n_passes, lambda e, m: store(m + NE))
            pool.wait_ge(zeros_stored, 16 * MAX_OVER)
            pool.wait_ge(rows_ready, 1)
            pool.wait_ge(w_low_done, n_passes * OVER + S_OVER)
            pool.sem_inc(passes_ended, 1)
            for r in range(2):
                for b in range(NB):
                    pool.indirect_dma_start(out=y_rows[:, 2 * r + b, :], out_offset=None, in_=y_dram[:, :],
                                            in_offset=bass.IndirectOffsetOnAxis(ap=row_i[:, r, b:b + 1], axis=0)
                                            ).then_inc(rows_fetched[2 * r + b], 16)

        @block.scalar
        def _(act):
            def high(s, i=None, per=0):
                act.wait_ge(landed[s % RAW_RING], at(i, per // RAW_RING * 16, 16 * (s // RAW_RING + 1)))
                if s >= PART_RING:
                    act.wait_ge(w_used, at(i, per, s - PART_RING + 1))
                act.activation(w_part[0][:, s % PART_RING, :], raw[:, s % RAW_RING, :], ACT.Copy).then_inc(w_high_done, 1)

            def norm(q, split=True):
                for b in range(NB):
                    act.wait_ge(x_loaded, 16) if q == 0 else act.wait_ge(x_added, 2 * (q - 1) + b + 1)
                    act.activation(h_td[:, b, :], xr[:, b, :], ACT.Square, accum_out=ss[:, q, b:b + 1]).then_inc(sq_done, 1)
                for b in range(NB):
                    act.wait_ge(sq_done, 2 * q + b + 1)
                    act.activation(rms[:, q, b:b + 1], ss[:, q, b:b + 1], ACT.Sqrt, scale=1.0 / D, bias=eps_t[:, :]).then_inc(rms_done, 1)
                for j in range(KC // 2):
                    act.wait_ge(h_turned, 4 * q + j + 1)
                    src = ps[:, j, :].rearrange("p (k t) -> p k t", k=2)
                    if split:
                        act.activation(hT[0][:, 2 * j:2 * j + 2, :], src, ACT.Copy).then_inc(hT_high_done, 1)
                    else:
                        act.activation(hT_plain[:, 2 * j:2 * j + 2, :], src, ACT.Copy).then_inc(hT_plain_done, 1)

            def front(l):
                b = S_FRONT[l]
                norm(2 * l)
                high(b + 3)
                high(b + 4)
                high(b + 5)
                act.wait_ge(w_used, b + 4)
                act.activation(sig, ps[:, 6:8, :].rearrange("p a (c t) -> p (a c) t", c=2), ACT.Sigmoid).then_inc(sig_done, 1)
                high(b + 6)
                high(b + 7)
                act.wait_ge(w_used, b + 6)
                act.activation(q_sq, ps[:, 0:2, :], ACT.Square).then_inc(qk_sq_done, 1)
                high(b + 8)
                act.wait_ge(w_used, b + 7)
                kv = ps[:, 2, :].rearrange("p (b n) -> p b n", b=NB)
                act.activation(k_sq, kv[:, :, 0:KVW], ACT.Square).then_inc(qk_sq_done, 1)
                act.activation(v_sb[:, :, :], kv[:, :, KVW:2 * KVW], ACT.Copy).then_inc(v_done, 1)
                act.wait_ge(qk_ss_done, 2 * l + 2)
                act.activation(qkr[:, :], qkss[:, :], ACT.Sqrt, scale=1.0 / HD, bias=eps_t[:, :]).then_inc(qk_rms_done, 1)
                high(b + 9)
                act.wait_ge(qk_turned, 2 * l + 1)
                act.activation(kT[:, :, :], ps[:, 3, :].rearrange("p (g t) -> p g t", g=NKV), ACT.Copy).then_inc(qkT_done, 1)
                act.wait_ge(qk_turned, 2 * l + 2)
                act.activation(qT[:, :, :], ps[:, 4:6, :].rearrange("p a (j t) -> p (a j) t", j=2), ACT.Copy).then_inc(qkT_done, 1)
                for t in range(NB):
                    act.wait_ge(max_done, NB * l + t + 1)
                    for h in range(NH):
                        act.activation(scores[t][:, h, :], scores[t][:, h, :], ACT.Exp, bias=mx[:, t, h:h + 1],
                                       accum_out=psums[:, t, h:h + 1]).then_inc(exp_done, 1)
                for m in range(3):
                    act.wait_ge(p_turned, 3 * l + m + 1)
                    bank = (4, 0, 2)[m]
                    act.activation(pT[:, m, :, :], ps[:, bank:bank + 2, :].rearrange("p a (h q) -> p (a h) q", h=4), ACT.Copy).then_inc(pT_done, 1)
                for t in range(NB):
                    act.wait_ge(pv_done, NB * l + t + 1)
                    act.activation(cat[0][:, 0:HP, t * P:(t + 1) * P], ps[:, 6 + t, :].rearrange("p (j q) -> p j q", j=HP), ACT.Copy).then_inc(cat_high_done, 1)
                high(b + 10)
                act.wait_ge(ln_step, 2 * l + 1)
                act.activation(ln_sq, cacc[:, :, :], ACT.Square).then_inc(ln_sq_done, 1)
                act.wait_ge(ln_sum, 2 * l + 2)
                act.activation(ln_sd, ps[:, 1, 0:S], ACT.Sqrt, bias=eps_t[:, :]).then_inc(ln_sd_done, 1)
                act.wait_ge(ln_step, 2 * l + 2)
                for c in range(CC):
                    act.activation(cacc[:, c, :], cacc[:, c, :], ACT.Silu, scale=pcol[:, l, c, TAPS + 1:TAPS + 2],
                                   bias=pcol[:, l, c, TAPS + 2:TAPS + 3]).then_inc(silu_c, 1)
                act.wait_ge(silu_c, CC * (l + 1))
                act.activation(cat[0][:, CC:2 * CC, :], cacc[:, :, :], ACT.Copy).then_inc(cat_high_done, 1)

            def gather_high(i, per, e):
                for j in range(2):
                    act.wait_ge(gathered, at(i, 2 * per, 2 * e + j + 1))
                    act.activation(xg[0][:, 4 * j:4 * j + 4, e % 2, :], ps[:, (3, 6)[j], :].rearrange("p (k c) -> p k c", k=4), ACT.Copy).then_inc(xg_high_done, 1)

            def expert_steps(s, n, e, experts, following, i, pers):
                per_s, per_n, per_e = pers
                for k in range(experts * EG):
                    last = k == experts * EG - 1 and not following
                    t = s + 6 * k
                    if not last:
                        high(t + 2, i, per_s)
                    act.wait_ge(act_turned, at(i, per_n, n + k + 1))
                    act.activation(act_part[0][:, k % 2, :], ps[:, 2, :], ACT.Copy).then_inc(act_high_done, 1)
                    if not last:
                        high(t + 3, i, per_s)
                        act.wait_ge(w_used, at(i, per_s, t + 2))
                        act.activation(silu_t, ps[:, 0, :], ACT.Silu).then_inc(silu_done, 1)
                        high(t + 4, i, per_s)
                        high(t + 5, i, per_s)
                        if k % EG == GATHER_AT and (k // EG + 1 < experts or following):
                            gather_high(i, per_e, e + k // EG + 1)
                        high(t + 6, i, per_s)
                        high(t + 7, i, per_s)
                    if k % EG == EG - 1:
                        x_ = e + k // EG
                        act.wait_ge(w_used, at(i, per_s, t + (2 if last else 6)))
                        act.wait_ge(y_free, at(i, per_e, x_ + 1))
                        act.activation(y_sb, ps[:, 4:6, :].rearrange("p a n -> p (a n)"), ACT.Copy).then_inc(y_copied, 1)

            act.wait_ge(dve_consts, DVE_CONSTS)
            act.sem_inc(y_copied, 1)
            for s in range(3):
                high(s)
            front(0)
            b = S_DENSE
            for j in range(3):
                high(b + j)
            norm(1)
            act.wait_ge(w_used, b + 1)
            act.activation(silu_t, ps[:, 0, :], ACT.Silu).then_inc(silu_done, 1)
            high(b + 3)
            act.wait_ge(prod_done, 1)
            act.activation(act_part[0][:, 0, :], prod_t, ACT.Copy).then_inc(act_high_done, 1)
            high(b + 4)
            with act.Fori(0, (DG - 1) // 2) as i:
                for u in range(2):
                    t = b + 2 + 3 * u
                    act.wait_ge(w_used, at(i, 6, t + 1))
                    act.activation(silu_t, ps[:, 2 * (1 - u), :], ACT.Silu).then_inc(silu_done, 1)
                    high(t + 3, i, 6)
                    high(t + 4, i, 6)
                    act.wait_ge(prod_done, at(i, 2, u + 2))
                    act.activation(act_part[0][:, 1 - u, :], prod_t, ACT.Copy).then_inc(act_high_done, 1)
                    high(t + 5, i, 6)
            high(S_FRONT[1] + 2)
            front(1)
            for j in range(3):
                high(S_MOE + j)
            norm(3, split=False)
            act.wait_ge(zdiff_done, 1)
            act.activation(zt[:, :], zt[:, :], ACT.Exp).then_inc(z_done, 1)
            n_passes = passes_in_all(act)
            gather_high(None, 0, 0)
            high(S_MOE + 3)
            act.wait_ge(w_used, S_MOE + 2)
            act.activation(silu_t, ps[:, 0, :], ACT.Silu).then_inc(silu_done, 1)
            high(S_MOE + 4)
            high(S_MOE + 5)
            with act.Fori(0, NE // 2 - 1) as i:
                expert_steps(S_MOE + 4, 0, 0, 2, True, i, (PAIR, 2 * EG, 2))
            expert_steps(S_MOE + 4 + (NE // 2 - 1) * PAIR, (NE - 2) * EG, NE - 2, 2, False, None, (0, 0, 0))

            def one_pass(e, m):
                for j in range(3):
                    high(S_OVER + j, m, OVER)
                gather_high(m, 1, NE)
                high(S_OVER + 3, m, OVER)
                act.wait_ge(w_used, at(m, OVER, S_OVER + 2))
                act.activation(silu_t, ps[:, 0, :], ACT.Silu).then_inc(silu_done, 1)
                high(S_OVER + 4, m, OVER)
                high(S_OVER + 5, m, OVER)
                expert_steps(S_OVER + 4, NE * EG, NE, 1, False, m, (OVER, EG, 1))

            overflow_passes(act, n_passes, one_pass)

        @block.vector
        def _(dve):
            steps = [0]

            def link(ins):
                steps[0] += 1
                ins.then_inc(dve_step, 1)
                dve.wait_ge(dve_step, steps[0])

            def low(s, i=None, per=0):
                dve.wait_ge(w_high_done, at(i, per, s + 1))
                r, q = s % RAW_RING, s % PART_RING
                dve.tensor_tensor(w_part[1][:, q, :], raw[:, r, :], w_part[0][:, q, :], ALU.subtract).then_inc(w_low_done, 1)

            def norm(q, split=True):
                for b in range(NB):
                    dve.wait_ge(rms_done, 2 * q + b + 1)
                    link(dve.reciprocal(rstd[:, q, b:b + 1], rms[:, q, b:b + 1]))
                    dve.wait_ge(gain_loaded[q % 2], 16 * (q // 2 + 1))
                    dve.scalar_tensor_tensor(out=h_td[:, b, :], in0=xr[:, b, :], scalar=rstd[:, q, b:b + 1],
                                             in1=gnorm[:, q % 2, :], op0=ALU.mult, op1=ALU.mult).then_inc(h_done, 1)
                if split:
                    for j in range(KC // 2):
                        dve.wait_ge(hT_high_done, 4 * q + j + 1)
                        dve.tensor_tensor(hT[1][:, 2 * j:2 * j + 2, :], ps[:, j, :].rearrange("p (k t) -> p k t", k=2),
                                          hT[0][:, 2 * j:2 * j + 2, :], ALU.subtract).then_inc(hT_low_done, 1)

            def conv(l, first, end):
                for tap in range(first, end):
                    for c in range(CC - 1):
                        n = (CC - 1) * (TAPS * l + tap) + c
                        w = pcol[:, l, c, tap:tap + 1]
                        src = hpad[:, c, tap:tap + S]
                        if tap == 0:
                            dve.tensor_scalar(cacc[:, c, :], src, w, pcol[:, l, c, TAPS:TAPS + 1],
                                              ALU.mult, ALU.add).then_inc(conv_dve, 1)
                        else:
                            dve.wait_ge(conv_dve, n - CC + 2)
                            dve.scalar_tensor_tensor(out=cacc[:, c, :], in0=src, scalar=w, in1=cacc[:, c, :],
                                                     op0=ALU.mult, op1=ALU.add).then_inc(conv_dve, 1)

            def add_to_x(used):
                dve.wait_ge(w_used, used)
                for b in range(NB):
                    dve.tensor_tensor(xr[:, b, :], xr[:, b, :], ps[:, 4 + 2 * b:6 + 2 * b, :].rearrange("p a n -> p (a n)"), ALU.add).then_inc(x_added, 1)

            def bias_and_max(l, t):
                n = P * (t + 1)
                dve.wait_ge(scored, NB * l + t + 1)
                banks = ps[:, 0:4, :] if t else ps[:, 6:8, :]
                raw_s = banks.rearrange("p a (h s) -> p (a h) s", s=n)
                for h in range(NH):
                    dve.scalar_tensor_tensor(out=scores[t][:, h, 0:n], in0=ndist[:, 2 * P - n:2 * P], scalar=2.0 ** (-8.0 * (h + 1) / NH),
                                             in1=raw_s[:, head_place(h), :], op0=ALU.mult, op1=ALU.add).then_inc(biased, 1)
                dve.tensor_copy(scores[t][:, :, n], sink_b[:, l, :]).then_inc(biased, 1)
                dve.wait_ge(biased, (NH + 1) * (NB * l + t + 1))
                link(dve.tensor_reduce(mx[:, t, :], scores[t], AX.X, ALU.max))
                dve.tensor_scalar(mx[:, t, :], mx[:, t, :], -1.0, None, ALU.mult).then_inc(max_done, 1)

            def normalise(l, t):
                n = P * (t + 1)
                dve.wait_ge(exp_done, NH * (NB * l + t + 1))
                link(dve.reciprocal(pinv[:, t, :], psums[:, t, :]))
                dve.tensor_tensor(scores[t][:, :, 0:n], scores[t][:, :, 0:n],
                                  pinv[:, t, :].unsqueeze(2).to_broadcast([P, NH, n]), ALU.mult).then_inc(probs_done, 1)

            def front(l):
                b = S_FRONT[l]
                norm(2 * l)
                for j in range(3, 6):
                    low(b + j)
                dve.wait_ge(sig_done, l + 1)
                dve.tensor_tensor(hpad[:, :, PAD:PAD + S], ps[:, 4:6, :].rearrange("p a (c t) -> p (a c) t", c=2), sig, ALU.mult).then_inc(glu_done, 1)
                dve.wait_ge(glu_done, l + 1)
                low(b + 6)
                conv(l, 0, 5)
                low(b + 7)
                conv(l, 5, 8)
                dve.wait_ge(qk_sq_done, 2 * l + 1)
                dve.tensor_reduce(qkss[:, 0:NB * NH], q_sq.rearrange("p b (h d) -> p (b h) d", d=HD), AX.X, ALU.add).then_inc(qk_ss_done, 1)
                low(b + 8)
                dve.wait_ge(qk_sq_done, 2 * l + 2)
                dve.tensor_reduce(qkss[:, NB * NH:], k_sq.rearrange("p b (h d) -> p (b h) d", d=HD), AX.X, ALU.add).then_inc(qk_ss_done, 1)
                dve.wait_ge(qk_rms_done, l + 1)
                link(dve.reciprocal(qkr[:, :], qkr[:, :]))
                kr = qkr[:, NB * NH:].rearrange("p (b g) -> p b g", b=NB).unsqueeze(3).to_broadcast([P, NB, NKV, HD])
                k_ps = ps[:, 2, :].rearrange("p (b m d) -> p b m d", b=NB, d=HD)[:, :, 0:NKV, :]
                link(dve.tensor_tensor(k_n.rearrange("p b (g d) -> p b g d", d=HD), k_ps, kr, ALU.mult))
                for r in range(2):
                    dve.tensor_tensor(kdup[:, :, :, r, :].rearrange("p b g d -> p (b g) d"), k_n.rearrange("p b (g d) -> p (b g) d", d=HD),
                                      qkg[:, l, 1, :].unsqueeze(1).to_broadcast([P, NB * NKV, HD]), ALU.mult).then_inc(qk_ready, 1)
                q3 = q_n.rearrange("p b (h d) -> p (b h) d", d=HD)
                link(dve.tensor_tensor(q3, ps[:, 0:2, :].rearrange("p b (h d) -> p (b h) d", d=HD),
                                       qkr[:, 0:NB * NH].unsqueeze(2).to_broadcast([P, NB * NH, HD]), ALU.mult))
                dve.tensor_tensor(q3, q3, qkg[:, l, 0, :].unsqueeze(1).to_broadcast([P, NB * NH, HD]), ALU.mult).then_inc(qk_ready, 1)
                low(b + 9)
                conv(l, 8, 16)
                bias_and_max(l, 0)
                bias_and_max(l, 1)
                conv(l, 16, 24)
                normalise(l, 0)
                normalise(l, 1)
                conv(l, 24, TAPS)
                for t in range(NB):
                    dve.wait_ge(cat_high_done, 3 * l + t + 1)
                    dve.tensor_tensor(cat[1][:, 0:HP, t * P:(t + 1) * P], ps[:, 6 + t, :].rearrange("p (j q) -> p j q", j=HP),
                                      cat[0][:, 0:HP, t * P:(t + 1) * P], ALU.subtract).then_inc(cat_low_done, 1)
                low(b + 10)
                dve.wait_ge(ln_sum, 2 * l + 1)
                dve.tensor_tensor(cacc[:, :, :], cacc[:, :, :], ps[:, 0, 0:S].unsqueeze(1).to_broadcast([P, CC, S]), ALU.subtract).then_inc(ln_step, 1)
                dve.wait_ge(ln_sd_done, l + 1)
                link(dve.reciprocal(ln_r, ln_sd))
                dve.tensor_tensor(cacc[:, :, :], cacc[:, :, :], ln_r.unsqueeze(1).to_broadcast([P, CC, S]), ALU.mult).then_inc(ln_step, 1)
                dve.wait_ge(cat_high_done, 3 * l + 3)
                dve.tensor_tensor(cat[1][:, CC:2 * CC, :], cacc[:, :, :], cat[0][:, CC:2 * CC, :], ALU.subtract).then_inc(cat_low_done, 1)

            def route():
                dve.wait_ge(routed, 1)
                link(dve.tensor_copy(lg[:, :, :], ps[:, 4, 0:NB * NE].rearrange("p (b e) -> p b e", b=NB)))
                for b in range(NB):
                    mine = lg[:, b, :].unsqueeze(2).to_broadcast([P, NE, NE])
                    other = lg[:, b, :].unsqueeze(1).to_broadcast([P, NE, NE])
                    link(dve.tensor_tensor(cmp_a[:, b], other, mine, ALU.is_gt))
                    link(dve.tensor_tensor(cmp_b[:, b], other, mine, ALU.is_equal))
                    link(dve.tensor_tensor(cmp_b[:, b], cmp_b[:, b], tri8[:, :, :], ALU.mult))
                    link(dve.tensor_tensor(cmp_a[:, b], cmp_a[:, b], cmp_b[:, b], ALU.add))
                link(dve.tensor_reduce(rank[:, :, :], cmp_a[:, :, :, :], AX.X, ALU.add))
                for r in range(2):
                    link(dve.tensor_scalar(selr[:, r], rank[:, :, :], float(r), None, ALU.is_equal))
                dve.tensor_tensor(sel[:, :, :], selr[:, 0], selr[:, 1], ALU.add).then_inc(sel_done, 1)
                for r in range(2):
                    link(dve.tensor_tensor(tmp8[:, r], selr[:, r], lg[:, :, :], ALU.mult))
                link(dve.tensor_reduce(top_l[:, :, :], tmp8[:, :, :, :], AX.X, ALU.add))
                dve.tensor_tensor(zt[:, :], top_l[:, 1], top_l[:, 0], ALU.subtract).then_inc(zdiff_done, 1)
                dve.wait_ge(counted, 1)
                link(dve.tensor_copy(pos[:, :, :], ps[:, 5, 0:NB * NE].rearrange("p (b e) -> p b e", b=NB)))
                link(dve.scalar_tensor_tensor(out=possel[:, :, :], in0=pos[:, :, :], scalar=1.0, in1=sel[:, :, :], op0=ALU.add, op1=ALU.mult))
                link(dve.tensor_scalar(possel[:, :, :], possel[:, :, :], -1.0, None, ALU.add))
                for b in range(NB):
                    dve.tensor_tensor(onehot[:, b], iota_c[:, :].unsqueeze(1).to_broadcast([P, NE, P]),
                                      possel[:, b, :].unsqueeze(2).to_broadcast([P, NE, P]), ALU.is_equal).then_inc(onehot_done, 1)
                link(dve.tensor_scalar(over_f[:, :], ps[:, 5, NB * NE:(NB + 1) * NE], float(P), None, ALU.is_gt))
                link(dve.tensor_copy(over_i[:, :], over_f[:, :]))
                link(dve.tensor_tensor(cmp_a[:, 0], tri8[:, :, :], over_f[:, :].unsqueeze(1).to_broadcast([P, NE, NE]), ALU.mult))
                link(dve.tensor_reduce(before_f[:, 0:NE], cmp_a[:, 0], AX.X, ALU.add))
                link(dve.tensor_reduce(before_f[:, NE:NE + 1], over_f[:, :], AX.X, ALU.add))
                dve.tensor_copy(before_i[:, :], before_f[:, :]).then_inc(over_ready, 1)
                link(dve.tensor_scalar(row_d[:, :], before_f[:, 0:NE], float(P), float(P * (NE - 1)), ALU.mult, ALU.add))
                link(dve.tensor_tensor(row_d[:, :], row_d[:, :], base_e[:, :], ALU.subtract))
                for b in range(NB):
                    link(dve.scalar_tensor_tensor(out=rank[:, b], in0=pos[:, b], scalar=float(P), in1=row_d[:, :], op0=ALU.is_ge, op1=ALU.mult))
                    link(dve.tensor_tensor(pos[:, b], pos[:, b], rank[:, b], ALU.add))
                    link(dve.tensor_tensor(pos[:, b], pos[:, b], base_e[:, :], ALU.add))
                for r in range(2):
                    link(dve.tensor_tensor(tmp8[:, r], selr[:, r], pos[:, :, :], ALU.mult))
                link(dve.tensor_reduce(row_f[:, :, :], tmp8[:, :, :, :], AX.X, ALU.add))
                dve.tensor_copy(row_i[:, :, :], row_f[:, :, :]).then_inc(rows_ready, 1)
                dve.wait_ge(z_done, 1)
                link(dve.tensor_scalar(den[:, :], zt[:, :], 1.0, None, ALU.add))
                link(dve.reciprocal(top_w[:, 0], den[:, :]))
                link(dve.tensor_tensor(top_w[:, 1], zt[:, :], top_w[:, 0], ALU.mult))

            def gather_low(i, per, e):
                for j in range(2):
                    dve.wait_ge(xg_high_done, at(i, 2 * per, 2 * e + j + 1))
                    dst = xg[1][:, 4 * j:4 * j + 4, e % 2, :]
                    dve.tensor_tensor(dst, ps[:, (3, 6)[j], :].rearrange("p (k c) -> p k c", k=4),
                                      xg[0][:, 4 * j:4 * j + 4, e % 2, :], ALU.subtract).then_inc(xg_low_done, 1)

            def expert_steps(s, n, e, experts, following, i, pers):
                per_s, per_n, per_e = pers
                for k in range(experts * EG):
                    last = k == experts * EG - 1 and not following
                    t = s + 6 * k
                    if not last:
                        low(t + 2, i, per_s)
                    dve.wait_ge(act_high_done, at(i, per_n, DG + n + k + 1))
                    dve.tensor_tensor(act_part[1][:, k % 2, :], ps[:, 2, :], act_part[0][:, k % 2, :], ALU.subtract).then_inc(act_low_done, 1)
                    if last:
                        continue
                    low(t + 3, i, per_s)
                    low(t + 4, i, per_s)
                    low(t + 5, i, per_s)
                    if k % EG == GATHER_AT and (k // EG + 1 < experts or following):
                        gather_low(i, per_e, e + k // EG + 1)
                    dve.wait_ge(w_used, at(i, per_s, t + 4))
                    dve.wait_ge(silu_done, at(i, per_n, DG + n + k + 2))
                    dve.tensor_tensor(prod_t, ps[:, 1, :], silu_t, ALU.mult).then_inc(prod_done, 1)
                    low(t + 6, i, per_s)
                    low(t + 7, i, per_s)

            dve.memset(ones[:, :], 1.0).then_inc(dve_consts, 1)
            dve.memset(mean_w[:, :], 1.0 / CW).then_inc(dve_consts, 1)
            dve.memset(eps_t[:, :], EPS).then_inc(dve_consts, 1)
            dve.memset(hpad[:, :, 0:PAD], 0.0).then_inc(dve_consts, 1)
            dve.memset(zero_r[:, :].bitcast(F32), 0.0).then_inc(dve_consts, 1)
            for s in range(3):
                low(s)
            dve.wait_ge(consts_loaded, CONST_LOADS)
            for l in range(L):
                dve.tensor_scalar(qkg[:, l, 0, :], qkg[:, l, 0, :], HD ** -0.5, None, ALU.mult).then_inc(dve_consts, 1)
            dve.wait_ge(prm_turned, 1)
            dve.tensor_copy(pcol[:, :, :, :].rearrange("p l c n -> p (l c n)"), ps[:, 7, 0:L * CC * NPRM]).then_inc(prm_ready, 1)
            dve.wait_ge(prm_ready, 1)
            dve.wait_ge(pool_consts, 14)
            dve.wait_ge(zeros_stored, 16 * MAX_OVER)
            dve.wait_ge(dve_consts, DVE_CONSTS + L)
            front(0)
            b = S_DENSE
            low(b)
            low(b + 1)
            add_to_x(b)
            low(b + 2)
            norm(1)
            low(b + 3)
            dve.wait_ge(w_used, b + 2)
            dve.wait_ge(silu_done, 1)
            dve.tensor_tensor(prod_t, ps[:, 1, :], silu_t, ALU.mult).then_inc(prod_done, 1)
            dve.wait_ge(act_high_done, 1)
            dve.tensor_tensor(act_part[1][:, 0, :], prod_t, act_part[0][:, 0, :], ALU.subtract).then_inc(act_low_done, 1)
            low(b + 4)
            with dve.Fori(0, (DG - 1) // 2) as i:
                for u in range(2):
                    t = b + 2 + 3 * u
                    low(t + 3, i, 6)
                    dve.wait_ge(w_used, at(i, 6, t + 2))
                    dve.wait_ge(silu_done, at(i, 2, u + 2))
                    dve.wait_ge(act_low_done, at(i, 2, u + 1))
                    dve.tensor_tensor(prod_t, ps[:, 2 * (1 - u) + 1, :], silu_t, ALU.mult).then_inc(prod_done, 1)
                    low(t + 4, i, 6)
                    dve.wait_ge(act_high_done, at(i, 2, u + 2))
                    dve.tensor_tensor(act_part[1][:, 1 - u, :], prod_t, act_part[0][:, 1 - u, :], ALU.subtract).then_inc(act_low_done, 1)
                    low(t + 5, i, 6)
            add_to_x(S_FRONT[1])
            low(S_FRONT[1] + 2)
            front(1)
            low(S_MOE)
            low(S_MOE + 1)
            add_to_x(S_MOE)
            low(S_MOE + 2)
            norm(3, split=False)
            route()
            n_passes = passes_in_all(dve)
            gather_low(None, 0, 0)
            low(S_MOE + 3)
            low(S_MOE + 4)
            dve.wait_ge(w_used, S_MOE + 4)
            dve.wait_ge(silu_done, DG + 1)
            dve.tensor_tensor(prod_t, ps[:, 1, :], silu_t, ALU.mult).then_inc(prod_done, 1)
            low(S_MOE + 5)
            with dve.Fori(0, NE // 2 - 1) as i:
                expert_steps(S_MOE + 4, 0, 0, 2, True, i, (PAIR, 2 * EG, 2))
            expert_steps(S_MOE + 4 + (NE // 2 - 1) * PAIR, (NE - 2) * EG, NE - 2, 2, False, None, (0, 0, 0))

            def one_pass(e, m):
                dve.tensor_scalar(pos[:, :, :], possel[:, :, :], -float(P), None, ALU.add).then_inc(shifted, 1)
                dve.wait_ge(shifted, m + 1)
                for b in range(NB):
                    dve.tensor_tensor(onehot[:, b], iota_c[:, :].unsqueeze(1).to_broadcast([P, NE, P]),
                                      pos[:, b, :].unsqueeze(2).to_broadcast([P, NE, P]), ALU.is_equal).then_inc(onehot_done, 1)
                for j in range(3):
                    low(S_OVER + j, m, OVER)
                gather_low(m, 1, NE)
                low(S_OVER + 3, m, OVER)
                low(S_OVER + 4, m, OVER)
                dve.wait_ge(w_used, at(m, OVER, S_OVER + 4))
                dve.wait_ge(silu_done, at(m, EG, DG + NE * EG + 1))
                dve.tensor_tensor(prod_t, ps[:, 1, :], silu_t, ALU.mult).then_inc(prod_done, 1)
                low(S_OVER + 5, m, OVER)
                expert_steps(S_OVER + 4, NE * EG, NE, 1, False, m, (OVER, EG, 1))

            overflow_passes(dve, n_passes, one_pass)
            for r in range(2):
                for b in range(NB):
                    dve.wait_ge(rows_fetched[2 * r + b], 16)
                    if r:
                        dve.wait_ge(combined, b + 1)
                    dve.scalar_tensor_tensor(out=xr[:, b, :], in0=y_rows[:, 2 * r + b, :], scalar=top_w[:, r, b:b + 1],
                                             in1=xr[:, b, :], op0=ALU.mult, op1=ALU.add).then_inc(combined, 1)

        @block.tensor
        def _(pe):
            def mm(out_, lhsT, rhs, start, stop=False):
                return pe.matmul(out_, lhsT, rhs, start=start, stop=stop, skip_group_check=True)

            def terms(out_, tokens, tidx, weights, widx, start, stop, weights_move=True):
                for n, (a, w) in enumerate(TERMS):
                    x_ = tokens[a][tidx]
                    w_ = weights[w][widx]
                    lhsT, rhs = (x_, w_) if weights_move else (w_, x_)
                    last = mm(out_, lhsT, rhs, start and n == 0, stop and n == 2)
                return last

            def slot(s, k, i=None, per=0):
                pe.wait_ge(w_low_done, at(i, per, s + 1))
                return [part_slot(0, s, k), part_slot(1, s, k)]

            def norm_turn(q):
                for b in range(NB):
                    pe.wait_ge(h_done, 2 * q + b + 1)
                    for k in range(KC):
                        last = pe.transpose(ps[:, k // 2, (k % 2) * S + b * P:(k % 2) * S + (b + 1) * P],
                                            h_td[:, b, k * P:(k + 1) * P], ident[:, :])
                        if b == 1 and k % 2:
                            last.then_inc(h_turned, 1)

            def front(l):
                b = S_FRONT[l]
                norm_turn(2 * l)
                for m in range(2):
                    for j in range(2):
                        w = slot(b + 2 * m + j, 4)
                        if m == 0:
                            pe.wait_ge(hT_low_done, 8 * l + 2 * j + 2)
                        for c in range(CC):
                            o = ps[:, 4 + 2 * m + c // 2, (c % 2) * S:(c % 2 + 1) * S]
                            for k in range(4):
                                last = terms(o, hT, (slice(None), 4 * j + k, slice(None)), w, (slice(None), k, slice(c * P, (c + 1) * P)),
                                             j == 0 and k == 0 and c % 2 == 0, j == 1 and k == 3, weights_move=False)
                        last.then_inc(w_used, 1)
                for j in range(2):
                    w = slot(b + 4 + j, 4)
                    for k in range(4):
                        for t in range(NB):
                            last = terms(ps[:, t, :], hT, (slice(None), 4 * j + k, slice(t * P, (t + 1) * P)), w, (slice(None), k, slice(None)),
                                         j == 0 and k == 0, j == 1 and k == 3)
                    last.then_inc(w_used, 1)
                w = slot(b + 6, 8)
                for k in range(8):
                    for t in range(NB):
                        last = terms(ps[:, 2, t * 2 * KVW:(t + 1) * 2 * KVW], hT, (slice(None), k, slice(t * P, (t + 1) * P)), w, (slice(None), k, slice(None)),
                                     k == 0 and t == 0, k == 7)
                last.then_inc(w_used, 1)
                pe.wait_ge(qk_ready, 3 * l + 2)
                for t in range(NB):
                    for g in range(NKV):
                        last = pe.transpose(ps[:, 3, g * S + t * P:g * S + (t + 1) * P], kdup[:, t, g].rearrange("p r d -> p (r d)"), ident[:, :])
                last.then_inc(qk_turned, 1)
                pe.wait_ge(qk_ready, 3 * l + 3)
                pe.wait_ge(glu_done, l + 1)
                for t in range(NB):
                    for j in range(HP):
                        last = pe.transpose(ps[:, 4 + j // 2, (j % 2) * S + t * P:(j % 2) * S + (t + 1) * P], q_n[:, t, j * P:(j + 1) * P], ident[:, :])
                last.then_inc(qk_turned, 1)
                pe.wait_ge(qkT_done, 2 * l + 2)
                pe.wait_ge(v_done, l + 1)
                for t in range(NB):
                    n = P * (t + 1)
                    per_bank = 512 // n
                    for h in range(NH):
                        r, m = h % 2, head_place(h)
                        o = ps[:, (0 if t else 6) + m // per_bank, (m % per_bank) * n:(m % per_bank + 1) * n]
                        last = mm(o, qT[r * HD:(r + 1) * HD, h // 2, t * P:(t + 1) * P], kT[r * HD:(r + 1) * HD, h // (NH // NKV), 0:n], True, True)
                    last.then_inc(scored, 1)
                for m, (t, kb, bank) in enumerate(((0, 0, 4), (1, 0, 0), (1, 1, 2))):
                    pe.wait_ge(probs_done, NB * l + t + 1)
                    for h in range(NH):
                        last = pe.transpose(ps[:, bank + h // 4, (h % 4) * P:(h % 4 + 1) * P], scores[t][:, h, kb * P:(kb + 1) * P], ident[:, :])
                    last.then_inc(p_turned, 1)
                for t in range(NB):
                    pe.wait_ge(pT_done, 3 * l + (1, 3)[t])
                    for g in range(NKV):
                        for r in range(2):
                            h0 = g * (NH // NKV) + r
                            o = ps[r * HD:(r + 1) * HD, 6 + t, 2 * g * P:(2 * g + 2) * P]
                            for kb in range(t + 1):
                                last = mm(o, v_sb[:, kb, g * HD:(g + 1) * HD], pT[:, t + kb, h0:h0 + 3:2, :], kb == 0, kb == t)
                    last.then_inc(pv_done, 1)
                def project(j):
                    w = slot(b + 7 + j, 2)
                    for k in range(2):
                        for t in range(NB):
                            for hf in range(2):
                                last = terms(ps[:, 4 + 2 * t + hf, :], cat, (slice(None), 2 * j + k, slice(t * P, (t + 1) * P)), w, (slice(None), k, slice(hf * 512, (hf + 1) * 512)),
                                             j == 0 and k == 0, j == 3 and k == 1)
                    last.then_inc(w_used, 1)
                pe.wait_ge(cat_low_done, 3 * l + 2)
                project(0)
                project(1)
                pe.wait_ge(conv_dve, (CC - 1) * TAPS * (l + 1))
                pe.wait_ge(conv_pool, 2 * TAPS * (l + 1))
                for c in range(CC):
                    last = mm(ps[:, 0, 0:S], mean_w[:, :], cacc[:, c, :], c == 0, c == CC - 1)
                last.then_inc(ln_sum, 1)
                pe.wait_ge(ln_sq_done, l + 1)
                for c in range(CC):
                    last = mm(ps[:, 1, 0:S], mean_w[:, :], ln_sq[:, c, :], c == 0, c == CC - 1)
                last.then_inc(ln_sum, 1)
                pe.wait_ge(cat_low_done, 3 * l + 3)
                project(2)
                project(3)

            def dense_gate_up(s, u, i=None):
                for m in range(2):
                    w = slot(s + m, 8, i, 6)
                    for f in range(2):
                        for k in range(KC):
                            last = terms(ps[:, 2 * u + m, f * S:(f + 1) * S], hT, (slice(None), k, slice(None)), w, (slice(None), k, slice(f * P, (f + 1) * P)),
                                         f == 0 and k == 0, k == KC - 1, weights_move=False)
                    last.then_inc(w_used, 1)

            def dense_down(s, u, start, stop, i=None):
                w = slot(s, 2, i, 6)
                a = [t[:, u, :].rearrange("p (f t) -> p f t", f=2) for t in act_part]
                for f in range(2):
                    for t in range(NB):
                        for hf in range(2):
                            last = terms(ps[:, 4 + 2 * t + hf, :], a, (slice(None), f, slice(t * P, (t + 1) * P)), w, (slice(None), f, slice(hf * 512, (hf + 1) * 512)),
                                         start and f == 0, stop and f == 1)
                last.then_inc(w_used, 1)

            def gather(i, per, e, e_reg):
                for j in range(2):
                    for k in range(4):
                        for b in range(NB):
                            last = mm(ps[:, (3, 6)[j], k * P:(k + 1) * P], h_td[:, b, (4 * j + k) * P:(4 * j + k + 1) * P],
                                      onehot[:, b, e_reg, :], k == 0 and b == 0, b == 1)
                    last.then_inc(gathered, 1)

            def gate_up(s, r, i, per):
                for m in range(2):
                    for j in range(2):
                        w = slot(s + 2 * m + j, 4, i, per)
                        for k in range(4):
                            last = terms(ps[:, m, :], xg, (slice(None), 4 * j + k, r, slice(None)), w, (slice(None), k, slice(None)),
                                         j == 0 and k == 0, j == 1 and k == 3)
                        last.then_inc(w_used, 1)

            def turn_act():
                for f in range(4):
                    last = pe.transpose(ps[:, 2, f * P:(f + 1) * P], prod_t[:, f * P:(f + 1) * P], ident[:, :])
                last.then_inc(act_turned, 1)

            def expert_steps(s, n, e, experts, following, i, pers, e_reg):
                per_s, per_n, per_e = pers
                for k in range(experts * EG):
                    last_step = k == experts * EG - 1 and not following
                    t = s + 6 * k
                    if not last_step:
                        pe.wait_ge(silu_done, at(i, per_n, DG + n + k + 1))
                        pe.wait_ge(prod_done, at(i, per_n, DG + n + k + 1))
                        nxt = (k + 1) // EG
                        if k % EG == EG - 1:
                            pe.wait_ge(xg_low_done, at(i, 2 * per_e, 2 * (e + nxt + 1)))
                        gate_up(t, (e + nxt) % 2, i, per_s)
                        if k % EG == GATHER_AT and (k // EG + 1 < experts or following):
                            gather(i, per_e, e + k // EG + 1, e_reg(k // EG + 1))
                    pe.wait_ge(act_low_done, at(i, per_n, DG + n + k + 1))
                    if k % EG == 0:
                        pe.wait_ge(y_copied, at(i, per_e, e + k // EG + 1))
                    for j in range(2):
                        w = slot(t + (0 if last_step else 4) + j, 2, i, per_s)
                        a = [p_[:, k % 2, :].rearrange("p (f c) -> p f c", f=4) for p_ in act_part]
                        for f in range(2):
                            for hf in range(2):
                                last = terms(ps[:, 4 + hf, :], a, (slice(None), 2 * j + f, slice(None)), w, (slice(None), f, slice(hf * 512, (hf + 1) * 512)),
                                             k % EG == 0 and j == 0 and f == 0, k % EG == EG - 1 and j == 1 and f == 1)
                        last.then_inc(w_used, 1)
                    if not last_step:
                        pe.wait_ge(prod_done, at(i, per_n, DG + n + k + 2))
                        turn_act()

            pe.wait_ge(pool_consts, 14)
            pe.wait_ge(dve_consts, DVE_CONSTS)
            pe.wait_ge(consts_loaded, CONST_LOADS)
            for l in range(L):
                for c in range(CC):
                    o = (l * CC + c) * NPRM
                    last = pe.transpose(ps[:, 7, o:o + NPRM], prm[:, l, c * P:(c + 1) * P], ident[0:NPRM, 0:NPRM])
            last.then_inc(prm_turned, 1)
            pe.wait_ge(prm_ready, 1)
            front(0)
            b = S_DENSE
            norm_turn(1)
            pe.wait_ge(hT_low_done, 8)
            dense_gate_up(b, 0)
            for bank in range(4, 8):
                mm(ps[:, bank, 0:P], zero_r[:, :], zero_r[:, :], True)
            with pe.Fori(0, (DG - 1) // 2) as i:
                for u in range(2):
                    t = b + 2 + 3 * u
                    dense_gate_up(t, 1 - u, i)
                    pe.wait_ge(act_low_done, at(i, 2, u + 1))
                    dense_down(t + 2, u, False, False, i)
            pe.wait_ge(act_low_done, DG)
            dense_down(S_FRONT[1] - 1, 0, False, True)
            front(1)
            norm_turn(3)
            pe.wait_ge(hT_plain_done, 4)
            for t in range(NB):
                for k in range(KC):
                    last = mm(ps[:, 4, t * NE:(t + 1) * NE], hT_plain[:, k, t * P:(t + 1) * P], wr[:, k, :], k == 0 and t == 0, k == KC - 1)
            last.then_inc(routed, 1)
            pe.wait_ge(sel_done, 1)
            mm(ps[:, 5, 0:NE], tri[:, :], sel[:, 0, :], True, True)
            mm(ps[:, 5, NE:2 * NE], tri[:, :], sel[:, 1, :], False)
            mm(ps[:, 5, NE:2 * NE], ones[:, :], sel[:, 0, :], False, True)
            mm(ps[:, 5, 2 * NE:3 * NE], ones[:, :], sel[:, 0, :], False)
            mm(ps[:, 5, 2 * NE:3 * NE], ones[:, :], sel[:, 1, :], False, True).then_inc(counted, 1)
            pe.wait_ge(onehot_done, 2)
            gather(None, 0, 0, 0)
            pe.wait_ge(xg_low_done, 2)
            n_passes = passes_in_all(pe)
            gate_up(S_MOE, 0, None, 0)
            pe.wait_ge(prod_done, DG + 1)
            turn_act()
            with pe.Fori(0, NE // 2 - 1) as i:
                expert_steps(S_MOE + 4, 0, 0, 2, True, i, (PAIR, 2 * EG, 2), lambda k: i * 2 + k)
            expert_steps(S_MOE + 4 + (NE // 2 - 1) * PAIR, (NE - 2) * EG, NE - 2, 2, False, None, (0, 0, 0), lambda k: NE - 2 + k)

            def one_pass(e, m):
                pe.wait_ge(onehot_done, at(m, 2, 4))
                gather(m, 1, NE, e)
                pe.wait_ge(silu_done, at(m, EG, DG + NE * EG))
                pe.wait_ge(prod_done, at(m, EG, DG + NE * EG))
                pe.wait_ge(xg_low_done, at(m, 2, 2 * (NE + 1)))
                gate_up(S_OVER, 0, m, OVER)
                pe.wait_ge(prod_done, at(m, EG, DG + NE * EG + 1))
                turn_act()
                expert_steps(S_OVER + 4, NE * EG, NE, 1, False, m, (OVER, EG, 1), None)

            overflow_passes(pe, n_passes, one_pass)


_INS = ["x", "attn_norm_g", "w_in", "q_norm_g", "k_norm_g", "sinks", "conv_w", "conv_b", "conv_ln_g", "conv_ln_b", "w_out",
        "ffn_norm_g", "dense_w_gate", "dense_w_up", "dense_w_down", "w_router", "moe_w_gate", "moe_w_up", "moe_w_down"]


def kernel(**inputs):
    import numpy as np
    import concourse.bacc as bacc
    from concourse.bass_utils import run_bass_kernel_spmd

    nc = bacc.Bacc("TRN2", target_bir_lowering=False, num_devices=1)
    arrays, args = {}, []
    for name in _INS:
        a = np.ascontiguousarray(inputs[name])
        arrays[f"in_{name}"] = a
        args.append(nc.dram_tensor(f"in_{name}", a.shape, mybir.dt.from_np(a.dtype), kind="ExternalInput").ap())
    args.append(nc.dram_tensor("out", inputs["x"].shape, F32, kind="ExternalOutput").ap())
    hybrid_trunk(nc, *args)
    r = run_bass_kernel_spmd(nc, [arrays], core_ids=[0])
    return r.results[0]["out"]
```

```python
from contextlib import ExitStack

import concourse.bass as bass
from concourse import mybir

F32 = mybir.dt.float32
F32R = mybir.dt.float32r
I32 = mybir.dt.int32
ALU = mybir.AluOpType
ACT = mybir.ActivationFunctionType
AX = mybir.AxisListType

P = 128
WINDOW = 128
RAW_RING = 6
PART_RING = 3
SLOT = 2048
TERMS = ((0, 0), (0, 1), (1, 0))


def hybrid_trunk(nc, x, attn_norm_g, w_in, q_norm_g, k_norm_g, sinks, conv_w, conv_b, conv_ln_g,
                 conv_ln_b, w_out, ffn_norm_g, dense_w_gate, dense_w_up, dense_w_down,
                 w_router, moe_w_gate, moe_w_up, moe_w_down, out):
    _, S, D = x.shape
    L, _, IN_W = w_in.shape
    HD = q_norm_g.shape[1]
    NH = sinks.shape[1]
    TAPS, CW = conv_w.shape[1], conv_w.shape[2]
    AW = NH * HD
    KVW = (IN_W - AW - 2 * CW) // 2
    NKV = KVW // HD
    DFF = dense_w_gate.shape[2]
    NE, EFF = moe_w_gate.shape[1], moe_w_gate.shape[3]
    NB = S // P
    KC = D // P
    CC = CW // P
    HP = NH // 2
    PAD = TAPS - 1
    EPS = 1e-6
    NPRM = TAPS + 3
    assert NB == 2 and KC == 8 and CC == 4 and HD == 64 and NKV == 2 and NH == 8 and L == 2

    FRONT_SLOTS = 11
    DG = DFF // 256
    EG = EFF // 512
    S_FRONT = [0, FRONT_SLOTS + 3 * DG]
    S_DENSE = FRONT_SLOTS
    S_MOE = S_FRONT[1] + FRONT_SLOTS
    PAIR = 6 * 2 * EG
    S_OVER = S_MOE + NE * EG * 6
    OVER = 6 * EG

    def at(i, per, const):
        return const if i is None else i * per + const

    with ExitStack() as ctx:
        def sb(name, shape, dt=F32):
            return ctx.enter_context(nc.sbuf_tensor(name, shape, dt))

        def sem(name):
            return ctx.enter_context(nc.semaphore(name))

        raw = sb("raw", [P, RAW_RING, SLOT])
        w_part = [sb("w_high", [P, PART_RING, SLOT], F32R), sb("w_low", [P, PART_RING, SLOT], F32R)]
        xr = sb("xr", [P, NB, D])
        h_td = sb("h_td", [P, NB, D])
        hT = [sb("hT_high", [P, KC, S], F32R), sb("hT_low", [P, KC, S], F32R)]
        cat = [sb("cat_high", [P, KC, S], F32R), sb("cat_low", [P, KC, S], F32R)]
        act_part = [sb("act_high", [P, 2, 512], F32R), sb("act_low", [P, 2, 512], F32R)]
        gnorm = sb("gnorm", [P, 2, D])
        hpad = sb("hpad", [P, CC, PAD + S])
        cacc = sb("cacc", [P, CC, S])
        v_sb = sb("v_sb", [P, NB, KVW])
        sc0 = sb("sc0", [P, NH, P + 1])
        work_a = sb("work_a", [P, 3072])
        work_b = sb("work_b", [P, NH * (2 * P + 1)])
        warm = sb("warm", [P, 2])
        ndist = sb("ndist", [P, 2 * P])
        ident = sb("ident", [P, P])
        ones = sb("ones", [P, P])
        mean_w = sb("mean_w", [P, P])
        tri = sb("tri", [P, P])
        pcol = sb("pcol", [P, L, CC, NPRM])
        qkg = sb("qkg", [P, 2, L])
        sink_b = sb("sink_b", [P, L, NH])
        eps_t = sb("eps_t", [P, 1])
        ss = sb("ss", [P, 4, NB])
        rms = sb("rms", [P, 4, NB])
        rstd = sb("rstd", [P, 4, NB])
        qkss = sb("qkss", [P, NB * (NH + NKV)])
        qkr = sb("qkr", [P, NB * (NH + NKV)])
        mx = sb("mx", [P, NB, NH])
        psums = sb("psums", [P, NB, NH])
        pinv = sb("pinv", [P, NB, NH])
        wr = sb("wr", [P, KC, NE])
        iota_c = sb("iota_c", [P, P])
        base_e = sb("base_e", [P, NE])
        base_ei = sb("base_ei", [P, NE], I32)
        tri8 = sb("tri8", [P, NE, NE])
        lg = sb("lg", [P, NB, NE])
        cmp_a = sb("cmp_a", [P, NB, NE, NE])
        cmp_b = sb("cmp_b", [P, NB, NE, NE])
        rank = sb("rank", [P, NB, NE])
        selr = sb("selr", [P, 2, NB, NE])
        sel = sb("sel", [P, NB, NE])
        possel = sb("possel", [P, NB, NE])
        pos = sb("pos", [P, NB, NE])
        tmp8 = sb("tmp8", [P, 2, NB, NE])
        top_l = sb("top_l", [P, 2, NB])
        top_w = sb("top_w", [P, 2, NB])
        zt = sb("zt", [P, NB])
        den = sb("den", [P, NB])
        row_d = sb("row_d", [P, NE])
        row_f = sb("row_f", [P, 2, NB])
        row_i = sb("row_i", [P, 2, NB], I32)
        over_f = sb("over_f", [P, NE])
        over_i = sb("over_i", [P, NE], I32)
        before_i = sb("before_i", [P, NE + 1], I32)
        before_f = sb("before_f", [P, NE + 1])
        ps = ctx.enter_context(nc.psum_tensor("ps", [P, 8, 512], F32))
        MAX_OVER = (2 * S) // (P + 1)
        y_dram = nc.dram_tensor("y_slots", ((NE + MAX_OVER) * P, D), F32, kind="Internal").ap()

        zero_r = sb("zero_r", [P, P], F32R)
        CONST_LOADS = 16 * 11
        DVE_CONSTS = 5
        GATHER_AT = 3

        h_flat = h_td[:, :, :].rearrange("p b d -> p (b d)")
        sig = h_flat[:, 0:CC * S].rearrange("p (c t) -> p c t", c=CC)
        q_n = h_flat[:, 0:NB * AW].rearrange("p (b n) -> p b n", b=NB)
        q_sq = h_flat[:, D:D + NB * AW].rearrange("p (b n) -> p b n", b=NB)
        ln_sq = sig
        ln_sd = h_flat[:, D:D + S]
        ln_r = h_flat[:, D + S:D + 2 * S]
        k_sq = work_a[:, 0:NB * KVW].rearrange("p (b n) -> p b n", b=NB)
        kdup = work_a[:, 512:1024].rearrange("p (b g r d) -> p b g r d", b=NB, g=NKV, r=2)
        kT = work_a[:, 1024:1536].rearrange("p (g t) -> p g t", g=NKV)
        qT = work_a[:, 2048:3072].rearrange("p (j t) -> p j t", j=HP)
        prm = work_b[0:NPRM, 0:L * CW].rearrange("n (l c) -> n l c", l=L)
        head_rows = work_b[0:2 * L, L * CW:L * CW + 2 * HD]
        HEAD_COLS = L * CC * NPRM
        pT = work_a[:, :].rearrange("p (m h q) -> p m h q", m=3, h=NH)
        sc1 = work_b[:, :].rearrange("p (h s) -> p h s", h=NH)
        scores = [sc0[:, :, :], sc1]
        onehot = work_b[:, 0:NB * NE * P].rearrange("p (b e c) -> p b e c", b=NB, e=NE)
        hT_plain = work_a[:, 0:KC * S].rearrange("p (k t) -> p k t", k=KC)
        y_sb = work_a[:, 0:D]
        silu_t = work_a[:, 2048:2560]
        prod_t = work_a[:, 2560:3072]
        xg = [t[:, :, :].rearrange("p k (r c) -> p k r c", r=2) for t in hT]
        y_rows = raw[:, 0:4, 0:D]

        products = [gnorm[:, m // 2, m % 2 * 2 * S:(m % 2 + 1) * 2 * S].rearrange("p (c t) -> p c t", c=2) for m in range(4)]

        x_loaded = [sem("x_loaded0"), sem("x_loaded1")]
        block0_projected = sem("block0_projected")
        ident_ready = sem("ident_ready")
        consts_loaded = sem("consts_loaded")
        gain_loaded = [sem("gain_loaded0"), sem("gain_loaded1")]
        landed = [sem(f"landed{i}") for i in range(RAW_RING)]
        slot_claimed = sem("slot_claimed")
        w_high_done = sem("w_high_done")
        w_low_done = sem("w_low_done")
        w_used = sem("w_used")
        pool_consts = sem("pool_consts")
        dve_consts = sem("dve_consts")
        prm_turned = sem("prm_turned")
        prm_ready = sem("prm_ready")
        sq_done = sem("sq_done")
        rms_done = sem("rms_done")
        rstd_done = sem("rstd_done")
        h_done = sem("h_done")
        h_turned = sem("h_turned")
        hT_high_done = sem("hT_high_done")
        hT_low_done = sem("hT_low_done")
        sig_done = sem("sig_done")
        glu_done = sem("glu_done")
        conv_dve = sem("conv_dve")
        conv_pool = sem("conv_pool")
        product_done = sem("product_done")
        qk_sq_done = sem("qk_sq_done")
        v_done = sem("v_done")
        qk_ss_done = sem("qk_ss_done")
        qk_rms_done = sem("qk_rms_done")
        qk_step = sem("qk_step")
        qk_turned = sem("qk_turned")
        qkT_done = sem("qkT_done")
        scored = sem("scored")
        biased = sem("biased")
        max_done = sem("max_done")
        exp_done = sem("exp_done")
        probs_done = sem("probs_done")
        dve_step = sem("dve_step")
        qk_ready = sem("qk_ready")
        p_turned = sem("p_turned")
        pT_done = sem("pT_done")
        pv_done = sem("pv_done")
        cat_high_done = sem("cat_high_done")
        cat_low_done = sem("cat_low_done")
        ln_sum = sem("ln_sum")
        ln_step = sem("ln_step")
        ln_sq_done = sem("ln_sq_done")
        ln_sd_done = sem("ln_sd_done")
        silu_c = sem("silu_c")
        x_added = sem("x_added")
        silu_done = sem("silu_done")
        prod_done = sem("prod_done")
        act_turned = sem("act_turned")
        act_high_done = sem("act_high_done")
        act_low_done = sem("act_low_done")
        hT_plain_done = sem("hT_plain_done")
        routed = sem("routed")
        sel_done = sem("sel_done")
        shifted = sem("shifted")
        zdiff_done = sem("zdiff_done")
        onehot_done = sem("onehot_done")
        rows_ready = sem("rows_ready")
        over_ready = sem("over_ready")
        z_done = sem("z_done")
        counted = sem("counted")
        gathered = sem("gathered")
        xg_high_done = sem("xg_high_done")
        xg_low_done = sem("xg_low_done")
        y_copied = sem("y_copied")
        y_stored = sem("y_stored")
        y_free = sem("y_free")
        zeros_stored = sem("zeros_stored")
        passes_ended = sem("passes_ended")
        rows_fetched = [sem(f"rows_fetched{i}") for i in range(4)]
        combined = sem("combined")
        out_stored = sem("out_stored")

        w_in_v = w_in.rearrange("l (k p) n -> l p k n", p=P)
        w_out_v = w_out.rearrange("l (k p) n -> l p k n", p=P)
        dg_v = dense_w_gate.rearrange("o (k p) f -> (o p) k f", p=P)
        du_v = dense_w_up.rearrange("o (k p) f -> (o p) k f", p=P)
        dd_v = dense_w_down.rearrange("o (k p) n -> (o p) k n", p=P)
        eg_v = moe_w_gate.rearrange("o e (k p) f -> (o e) p k f", p=P)
        eu_v = moe_w_up.rearrange("o e (k p) f -> (o e) p k f", p=P)
        ed_v = moe_w_down.rearrange("o e (k p) n -> (o e) p k n", p=P)
        x_v = x.rearrange("o (b p) d -> p (o b) d", p=P)
        out_v = out.rearrange("o (b p) d -> p (o b) d", p=P)
        VAL, GATE = AW + 2 * KVW, AW + 2 * KVW + CW

        def passes_in_all(eng):
            eng.wait_ge(over_ready, 1)
            return eng.value_load(before_i[0:1, NE:NE + 1], min_val=0, max_val=MAX_OVER)

        def overflow_passes(eng, n_passes, one_pass):
            with eng.If(n_passes > 0):
                with eng.Fori(0, NE) as e:
                    over = eng.value_load(over_i[0:1, bass.ds(e, 1)], min_val=0, max_val=1)
                    with eng.If(over > 0):
                        m = eng.value_load(before_i[0:1, bass.ds(e, 1)], min_val=0, max_val=MAX_OVER - 1)
                        one_pass(e, m)
                eng.sem_inc(passes_ended, 1)

        def head_place(h):
            return h % 2 * (NH // 2) + h // 2

        def raw_slot(s, k):
            return raw[:, s % RAW_RING, :].rearrange("p (k n) -> p k n", k=k)

        def part_slot(part, s, k):
            return w_part[part][:, s % PART_RING, :].rearrange("p (k n) -> p k n", k=k)

        block = ctx.enter_context(nc.Block())

        @block.sync
        def _(sp):
            def load(s, src, k, i=None, per=0):
                if s >= RAW_RING:
                    sp.wait_ge(w_low_done, at(i, per, s - RAW_RING + 1))
                if i is not None:
                    sp.sem_inc(slot_claimed, 1)
                sp.dma_start(raw_slot(s, k), src).then_inc(landed[s % RAW_RING], 16)

            def front(l):
                b = S_FRONT[l]
                for n, col in enumerate((VAL, GATE, 0)):
                    for j in range(2):
                        load(b + 2 * n + j, w_in_v[l, :, 4 * j:4 * j + 4, col:col + 512], 4)
                    if l == 0 and n == 0:
                        constants()
                load(b + 6, w_in_v[l, :, :, AW:AW + 2 * KVW], 8)
                for j in range(4):
                    load(b + 7 + j, w_out_v[l, :, 2 * j:2 * j + 2, :], 2)

            def dense_gate_up(s, col, i=None):
                load(s, dg_v[:, :, bass.ds(col, 256)], 8, i, 6)
                load(s + 1, du_v[:, :, bass.ds(col, 256)], 8, i, 6)

            def dense_down(s, row, i=None):
                load(s, dd_v[:, bass.ds(row, 2), :], 2, i, 6)

            def gate_up(s, e, g, i, per):
                for n, v in enumerate((eg_v, eu_v)):
                    for j in range(2):
                        load(s + 2 * n + j, v[e, :, 4 * j:4 * j + 4, 512 * g:512 * g + 512], 4, i, per)

            def down(s, e, g, i, per):
                for j in range(2):
                    load(s + j, ed_v[e, :, 4 * g + 2 * j:4 * g + 2 * j + 2, :], 2, i, per)

            def expert_steps(s, experts, following, i, per):
                groups = [(e, g) for e in experts for g in range(EG)]
                for n, (e, g) in enumerate(groups):
                    after = groups[n + 1] if n + 1 < len(groups) else following
                    if after is not None:
                        gate_up(s + 6 * n, *after, i, per)
                    down(s + 6 * n + (4 if after is not None else 0), e, g, i, per)

            def bcast(ap):
                return ap.partition_broadcast(P)

            def constants():
                sp.dma_start(prm[0:TAPS, :, :], conv_w.rearrange("l k c -> k l c")).then_inc(consts_loaded, 16)
                for r, v in enumerate((conv_b, conv_ln_g, conv_ln_b)):
                    sp.dma_start(prm[TAPS + r:TAPS + r + 1, :, :], v.rearrange("(o l) c -> o l c", o=1)).then_inc(consts_loaded, 16)
                for r in range(2):
                    for n, g in enumerate((q_norm_g, k_norm_g)):
                        sp.dma_start(head_rows[n * L:(n + 1) * L, r * HD:(r + 1) * HD], g).then_inc(consts_loaded, 16)
                for l in range(L):
                    sp.dma_start(sink_b[:, l, :], bcast(sinks[l])).then_inc(consts_loaded, 16)
                sp.dma_start(wr[:, :, :], w_router.rearrange("o (k p) e -> p (o k) e", p=P)).then_inc(consts_loaded, 16)

            sp.dma_start(xr[:, 0, :], x_v[:, 0, :]).then_inc(x_loaded[0], 16)
            sp.dma_start(gnorm[:, 0, :], bcast(attn_norm_g[0])).then_inc(gain_loaded[0], 16)
            sp.dma_start(xr[:, 1, :], x_v[:, 1, :]).then_inc(x_loaded[1], 16)
            front(0)
            dense_gate_up(S_DENSE, 0)
            with sp.Fori(0, (DG - 1) // 2) as i:
                for u in range(2):
                    dense_gate_up(S_DENSE + 2 + 3 * u, i * 512 + 256 * (u + 1), i)
                    dense_down(S_DENSE + 4 + 3 * u, i * 4 + 2 * u, i)
            dense_down(S_DENSE + 3 * DG - 1, 2 * (DG - 1))
            sp.wait_ge(h_done, 4)
            sp.dma_start(gnorm[:, 0, :], bcast(attn_norm_g[1])).then_inc(gain_loaded[0], 16)
            front(1)
            gate_up(S_MOE, 0, 0, None, 0)

            def one_pass(e, m):
                gate_up(S_OVER, e, 0, m, OVER)
                expert_steps(S_OVER + 4, (e,), None, m, OVER)

            with sp.Fori(0, NE // 2 - 1) as i:
                expert_steps(S_MOE + 4, (i * 2, i * 2 + 1), (i * 2 + 2, 0), i, PAIR)
            expert_steps(S_MOE + 4 + (NE // 2 - 1) * PAIR, (NE - 2, NE - 1), None, None, 0)
            overflow_passes(sp, passes_in_all(sp), one_pass)
            for t in range(NB):
                sp.wait_ge(combined, 2 * t + 2)
                sp.dma_start(out_v[:, t, :], xr[:, t, :]).then_inc(out_stored, 16)
            sp.wait_ge(out_stored, 16 * NB)

        @block.gpsimd
        def _(pool):
            pool.sem_inc(y_free, 1)
            pool.memset(ident[:, :], 0.0).then_inc(ident_ready, 1)
            pool.wait_ge(ident_ready, 1)
            pool.affine_select(out=ident[:, :], in_=ident[:, :], compare_op=ALU.not_equal, fill=1.0, base=0,
                               pattern=[[-1, P]], channel_multiplier=1).then_inc(ident_ready, 1)
            pool.memset(tri[:, :], 1.0).then_inc(pool_consts, 1)
            pool.memset(tri8[:, :, :], 1.0).then_inc(pool_consts, 1)
            pool.iota(iota_c[:, :].bitcast(I32), pattern=[[1, P]], base=0, channel_multiplier=0).then_inc(pool_consts, 1)
            pool.iota(base_ei[:, :], pattern=[[P, NE]], base=0, channel_multiplier=0).then_inc(pool_consts, 1)
            pool.iota(ndist[:, :].bitcast(I32), pattern=[[1, 2 * P]], base=-P, channel_multiplier=-1).then_inc(pool_consts, 1)
            pool.wait_ge(pool_consts, 5)
            pool.affine_select(out=tri[:, :], in_=tri[:, :], compare_op=ALU.is_ge, fill=0.0, base=-1,
                               pattern=[[1, P]], channel_multiplier=-1).then_inc(pool_consts, 1)
            pool.affine_select(out=tri8[:, :, :], in_=tri8[:, :, :], compare_op=ALU.is_ge, fill=0.0, base=-1,
                               pattern=[[1, NE], [-1, NE]], channel_multiplier=0).then_inc(pool_consts, 1)
            pool.tensor_copy(iota_c[:, :], iota_c[:, :].bitcast(I32)).then_inc(pool_consts, 1)
            pool.tensor_copy(base_e[:, :], base_ei[:, :]).then_inc(pool_consts, 1)
            pool.tensor_copy(ndist[:, :], ndist[:, :].bitcast(I32)).then_inc(pool_consts, 1)
            pool.wait_ge(pool_consts, 10)
            pool.affine_select(out=ndist[:, :], in_=ndist[:, :], compare_op=ALU.is_ge, fill=-1e30, base=P,
                               pattern=[[-1, 2 * P]], channel_multiplier=1).then_inc(pool_consts, 1)
            pool.wait_ge(pool_consts, 11)
            pool.affine_select(out=ndist[:, :], in_=ndist[:, :], compare_op=ALU.is_ge, fill=-1e30, base=WINDOW - 1 - P,
                               pattern=[[1, 2 * P]], channel_multiplier=-1).then_inc(pool_consts, 1)

            def conv(l):
                for tap in range(1, TAPS):
                    n = TAPS * l + tap
                    pool.wait_ge(product_done, 2 * (n + 1))
                    if tap > 1:
                        pool.wait_ge(conv_pool, n - 1 - l)
                    pool.tensor_tensor(cacc[:, 2:4, :], cacc[:, 2:4, :], products[tap % 4], ALU.add).then_inc(conv_pool, 1)
                pool.wait_ge(conv_pool, (TAPS - 1) * (l + 1))
                pool.dma_start(gnorm[:, 1, :], ffn_norm_g[l].partition_broadcast(P)).then_inc(gain_loaded[1], 16)

            conv(0)
            pool.wait_ge(cat_low_done, 4)
            pool.memset(cacc[:, :, :], 0.0).then_inc(pool_consts, 1)
            pool.wait_ge(pool_consts, 13)
            for m in range(MAX_OVER):
                pool.dma_start(y_dram[(NE + m) * P:(NE + m + 1) * P, :], cacc[:, :, :].rearrange("p c t -> p (c t)")).then_inc(zeros_stored, 16)
            pool.wait_ge(zeros_stored, 16 * MAX_OVER)
            conv(1)
            n_passes = passes_in_all(pool)

            def store(m):
                pool.wait_ge(y_copied, m + 2)
                pool.dma_start(y_dram[bass.ds(m * P, P), :], y_sb).then_inc(y_stored, 16)
                pool.wait_ge(y_stored, (m + 1) * 16)
                pool.sem_inc(y_free, 1)

            with pool.Fori(0, NE) as e:
                store(e)
            overflow_passes(pool, n_passes, lambda e, m: store(m + NE))
            pool.wait_ge(rows_ready, 1)
            pool.wait_ge(w_low_done, n_passes * OVER + S_OVER)
            pool.sem_inc(passes_ended, 1)
            for b in range(NB):
                for r in range(2):
                    pool.indirect_dma_start(out=y_rows[:, 2 * r + b, :], out_offset=None, in_=y_dram[:, :],
                                            in_offset=bass.IndirectOffsetOnAxis(ap=row_i[:, r, b:b + 1], axis=0)
                                            ).then_inc(rows_fetched[2 * r + b], 16)

        @block.scalar
        def _(act):
            def high(s, i=None, per=0):
                act.wait_ge(landed[s % RAW_RING], at(i, per // RAW_RING * 16, 16 * (s // RAW_RING + 1)))
                if s >= PART_RING:
                    act.wait_ge(w_used, at(i, per, s - PART_RING + 1))
                act.activation(w_part[0][:, s % PART_RING, :], raw[:, s % RAW_RING, :], ACT.Copy).then_inc(w_high_done, 1)

            def norm(q, slots, split=True):
                for b in range(NB):
                    if q == 0:
                        act.wait_ge(x_loaded[b], 16)
                    else:
                        act.wait_ge(x_added, 2 * (q - 1) + b + 1)
                    act.activation(h_td[:, b, :], xr[:, b, :], ACT.Square, accum_out=ss[:, q, b:b + 1]).then_inc(sq_done, 1)
                    act.wait_ge(sq_done, 2 * q + b + 1)
                    act.activation(rms[:, q, b:b + 1], ss[:, q, b:b + 1], ACT.Sqrt, scale=1.0 / D, bias=eps_t[:, :]).then_inc(rms_done, 1)
                for j in range(KC // 2):
                    if j % 2 == 0 and j // 2 < len(slots):
                        high(slots[j // 2])
                    act.wait_ge(h_turned, 4 * q + j + 1)
                    src = ps[:, j, :].rearrange("p (k t) -> p k t", k=2)
                    if split:
                        act.activation(hT[0][:, 2 * j:2 * j + 2, :], src, ACT.Copy).then_inc(hT_high_done, 1)
                    else:
                        act.activation(hT_plain[:, 2 * j:2 * j + 2, :], src, ACT.Copy).then_inc(hT_plain_done, 1)

            def multiply(l, first, end):
                for tap in range(first, end):
                    if tap > 4:
                        act.wait_ge(conv_pool, (TAPS - 1) * l + tap - 4)
                    for c in range(2, CC):
                        w = pcol[:, l, c, tap:tap + 1]
                        src = hpad[:, c, tap:tap + S]
                        if tap == 0:
                            act.activation(cacc[:, c, :], src, ACT.Identity, scale=w, bias=pcol[:, l, c, TAPS:TAPS + 1]).then_inc(product_done, 1)
                        else:
                            act.activation(products[tap % 4][:, c - 2, :], src, ACT.Copy, scale=w).then_inc(product_done, 1)

            def load_table(function):
                act.activation(warm[:, 0:1], eps_t[:, :], function)

            def front(l):
                b = S_FRONT[l]
                if l == 0:
                    norm(0, (0, 1))
                    high(2)
                else:
                    norm(2, (b + 2,))
                high(b + 3)
                high(b + 4)
                high(b + 5)
                act.wait_ge(w_used, b + 4)
                act.activation(sig, ps[:, 6:8, :].rearrange("p a (c t) -> p (a c) t", c=2), ACT.Sigmoid).then_inc(sig_done, 1)
                high(b + 6)
                act.wait_ge(glu_done, l + 1)
                if l == 0:
                    act.wait_ge(prm_ready, 3)
                else:
                    act.wait_ge(zeros_stored, 16 * MAX_OVER)
                multiply(l, 0, 5)
                high(b + 7)
                act.wait_ge(w_used, b + 6)
                act.activation(q_sq, ps[:, 0:2, :], ACT.Square).then_inc(qk_sq_done, 1)
                multiply(l, 5, 8)
                load_table(ACT.Sqrt)
                act.wait_ge(w_used, b + 7)
                kv = ps[:, 2, :].rearrange("p (b n) -> p b n", b=NB)
                act.activation(k_sq, kv[:, :, 0:KVW], ACT.Square).then_inc(qk_sq_done, 1)
                act.wait_ge(qk_ss_done, 2 * l + 2)
                act.activation(qkr[:, :], qkss[:, :], ACT.Sqrt, scale=1.0 / HD, bias=eps_t[:, :]).then_inc(qk_rms_done, 1)
                multiply(l, 8, 10)
                multiply(l, 10, 11)
                act.wait_ge(qk_turned, 2 * l + 1)
                act.activation(kT[:, :, :], ps[:, 3, :].rearrange("p (g t) -> p g t", g=NKV), ACT.Copy, scale=qkg[:, 1, l:l + 1]).then_inc(qkT_done, 1)
                act.activation(v_sb[:, :, :], kv[:, :, KVW:2 * KVW], ACT.Copy).then_inc(v_done, 1)
                multiply(l, 11, 12)
                act.wait_ge(qk_turned, 2 * l + 2)
                act.activation(qT[:, :, :], ps[:, 4:6, :].rearrange("p a (j t) -> p (a j) t", j=2), ACT.Copy, scale=qkg[:, 0, l:l + 1]).then_inc(qkT_done, 1)
                multiply(l, 12, 16)
                high(b + 8)
                multiply(l, 16, 21)
                load_table(ACT.Exp)
                for t in range(NB):
                    if t:
                        multiply(l, 21, 26)
                    act.wait_ge(max_done, NB * l + t + 1)
                    for h in range(NH):
                        act.activation(scores[t][:, h, :], scores[t][:, h, :], ACT.Exp, bias=mx[:, t, h:h + 1],
                                       accum_out=psums[:, t, h:h + 1]).then_inc(exp_done, 1)
                for m in range(3):
                    act.wait_ge(p_turned, 3 * l + m + 1)
                    bank = (4, 0, 2)[m]
                    act.activation(pT[:, m, :, :], ps[:, bank:bank + 2, :].rearrange("p a (h q) -> p (a h) q", h=4), ACT.Copy).then_inc(pT_done, 1)
                    if m == 0:
                        multiply(l, 26, TAPS)
                for t in range(NB):
                    act.wait_ge(pv_done, NB * l + t + 1)
                    act.activation(cat[0][:, 0:HP, t * P:(t + 1) * P], ps[:, 6 + t, :].rearrange("p (j q) -> p j q", j=HP), ACT.Copy).then_inc(cat_high_done, 1)
                high(b + 9)
                load_table(ACT.Sqrt)
                act.wait_ge(ln_step, 2 * l + 1)
                act.activation(ln_sq, cacc[:, :, :], ACT.Square).then_inc(ln_sq_done, 1)
                act.wait_ge(ln_sum, 2 * l + 2)
                act.activation(ln_sd, ps[:, 1, 0:S], ACT.Sqrt, bias=eps_t[:, :]).then_inc(ln_sd_done, 1)
                high(b + 10)
                load_table(ACT.Silu)
                act.wait_ge(ln_step, 2 * l + 2)
                for c in range(CC):
                    act.activation(cacc[:, c, :], cacc[:, c, :], ACT.Silu, scale=pcol[:, l, c, TAPS + 1:TAPS + 2],
                                   bias=pcol[:, l, c, TAPS + 2:TAPS + 3]).then_inc(silu_c, 1)
                    if c % 2:
                        act.wait_ge(silu_c, CC * l + c + 1)
                        act.activation(cat[0][:, CC + c - 1:CC + c + 1, :], cacc[:, c - 1:c + 1, :], ACT.Copy).then_inc(cat_high_done, 1)
                load_table(ACT.Sqrt)

            def gather_high(i, per, e):
                for j in range(2):
                    act.wait_ge(gathered, at(i, 2 * per, 2 * e + j + 1))
                    act.activation(xg[0][:, 4 * j:4 * j + 4, e % 2, :], ps[:, (3, 6)[j], :].rearrange("p (k c) -> p k c", k=4), ACT.Copy).then_inc(xg_high_done, 1)

            def expert_steps(s, n, e, experts, following, i, pers):
                per_s, per_n, per_e = pers
                for k in range(experts * EG):
                    last = k == experts * EG - 1 and not following
                    t = s + 6 * k
                    if not last:
                        high(t + 2, i, per_s)
                    act.wait_ge(act_turned, at(i, per_n, n + k + 1))
                    act.activation(act_part[0][:, k % 2, :], ps[:, 2, :], ACT.Copy).then_inc(act_high_done, 1)
                    if not last:
                        high(t + 3, i, per_s)
                        act.wait_ge(w_used, at(i, per_s, t + 2))
                        act.activation(silu_t, ps[:, 0, :], ACT.Silu).then_inc(silu_done, 1)
                        high(t + 4, i, per_s)
                        high(t + 5, i, per_s)
                        if k % EG == GATHER_AT and (k // EG + 1 < experts or following):
                            gather_high(i, per_e, e + k // EG + 1)
                        high(t + 6, i, per_s)
                        high(t + 7, i, per_s)
                    if k % EG == EG - 1:
                        x_ = e + k // EG
                        act.wait_ge(w_used, at(i, per_s, t + (2 if last else 6)))
                        act.wait_ge(y_free, at(i, per_e, x_ + 1))
                        act.activation(y_sb, ps[:, 4:6, :].rearrange("p a n -> p (a n)"), ACT.Copy).then_inc(y_copied, 1)

            act.wait_ge(dve_consts, 1)
            act.sem_inc(y_copied, 1)
            front(0)
            b = S_DENSE
            high(b)
            high(b + 1)
            norm(1, (b + 2,))
            act.wait_ge(w_used, b + 1)
            act.activation(silu_t, ps[:, 0, :], ACT.Silu).then_inc(silu_done, 1)
            high(b + 3)
            act.wait_ge(prod_done, 1)
            act.activation(act_part[0][:, 0, :], prod_t, ACT.Copy).then_inc(act_high_done, 1)
            high(b + 4)
            with act.Fori(0, (DG - 1) // 2) as i:
                for u in range(2):
                    t = b + 2 + 3 * u
                    act.wait_ge(w_used, at(i, 6, t + 1))
                    act.activation(silu_t, ps[:, 2 * (1 - u), :], ACT.Silu).then_inc(silu_done, 1)
                    high(t + 3, i, 6)
                    high(t + 4, i, 6)
                    act.wait_ge(prod_done, at(i, 2, u + 2))
                    act.activation(act_part[0][:, 1 - u, :], prod_t, ACT.Copy).then_inc(act_high_done, 1)
                    high(t + 5, i, 6)
            front(1)
            for j in range(2):
                high(S_MOE + j)
            norm(3, (S_MOE + 2,), split=False)
            act.wait_ge(zdiff_done, 1)
            act.activation(zt[:, :], zt[:, :], ACT.Exp).then_inc(z_done, 1)
            gather_high(None, 0, 0)
            high(S_MOE + 3)
            n_passes = passes_in_all(act)
            act.wait_ge(w_used, S_MOE + 2)
            act.activation(silu_t, ps[:, 0, :], ACT.Silu).then_inc(silu_done, 1)
            high(S_MOE + 4)
            high(S_MOE + 5)
            with act.Fori(0, NE // 2 - 1) as i:
                expert_steps(S_MOE + 4, 0, 0, 2, True, i, (PAIR, 2 * EG, 2))
            expert_steps(S_MOE + 4 + (NE // 2 - 1) * PAIR, (NE - 2) * EG, NE - 2, 2, False, None, (0, 0, 0))

            def one_pass(e, m):
                for j in range(3):
                    high(S_OVER + j, m, OVER)
                gather_high(m, 1, NE)
                high(S_OVER + 3, m, OVER)
                act.wait_ge(w_used, at(m, OVER, S_OVER + 2))
                act.activation(silu_t, ps[:, 0, :], ACT.Silu).then_inc(silu_done, 1)
                high(S_OVER + 4, m, OVER)
                high(S_OVER + 5, m, OVER)
                expert_steps(S_OVER + 4, NE * EG, NE, 1, False, m, (OVER, EG, 1))

            overflow_passes(act, n_passes, one_pass)

        @block.vector
        def _(dve):
            steps = [0]

            def link(ins):
                steps[0] += 1
                ins.then_inc(dve_step, 1)
                dve.wait_ge(dve_step, steps[0])

            def low(s, i=None, per=0):
                dve.wait_ge(w_high_done, at(i, per, s + 1))
                r, q = s % RAW_RING, s % PART_RING
                dve.tensor_tensor(w_part[1][:, q, :], raw[:, r, :], w_part[0][:, q, :], ALU.subtract).then_inc(w_low_done, 1)

            def norm(q, slots, split=True):
                if q > 0:
                    for b in range(NB):
                        if b == 0:
                            dve.wait_ge(block0_projected, q)
                        else:
                            dve.wait_ge(w_used, (S_DENSE, S_FRONT[1], S_MOE)[q - 1])
                        dve.tensor_tensor(xr[:, b, :], xr[:, b, :], ps[:, 4 + 2 * b:6 + 2 * b, :].rearrange("p a n -> p (a n)"), ALU.add).then_inc(x_added, 1)
                for b in range(NB):
                    dve.wait_ge(rms_done, 2 * q + b + 1)
                    link(dve.reciprocal(rstd[:, q, b:b + 1], rms[:, q, b:b + 1]))
                    dve.wait_ge(gain_loaded[q % 2], 16 * (q // 2 + 1))
                    dve.scalar_tensor_tensor(out=h_td[:, b, :], in0=xr[:, b, :], scalar=rstd[:, q, b:b + 1],
                                             in1=gnorm[:, q % 2, :], op0=ALU.mult, op1=ALU.mult).then_inc(h_done, 1)
                if split:
                    for j in range(KC // 2):
                        if q == 0 and j % 2 == 0:
                            low(slots[j // 2])
                        dve.wait_ge(hT_high_done, 4 * q + j + 1)
                        dve.tensor_tensor(hT[1][:, 2 * j:2 * j + 2, :], ps[:, j, :].rearrange("p (k t) -> p k t", k=2),
                                          hT[0][:, 2 * j:2 * j + 2, :], ALU.subtract).then_inc(hT_low_done, 1)
                if q > 0:
                    for slot in slots:
                        low(slot)

            def conv(l, first, end):
                for tap in range(first, end):
                    for c in range(2):
                        n = 2 * (TAPS * l + tap) + c
                        w = pcol[:, l, c, tap:tap + 1]
                        src = hpad[:, c, tap:tap + S]
                        if tap == 0:
                            dve.tensor_scalar(cacc[:, c, :], src, w, pcol[:, l, c, TAPS:TAPS + 1],
                                              ALU.mult, ALU.add).then_inc(conv_dve, 1)
                        else:
                            dve.wait_ge(conv_dve, n - 1)
                            dve.scalar_tensor_tensor(out=cacc[:, c, :], in0=src, scalar=w, in1=cacc[:, c, :],
                                                     op0=ALU.mult, op1=ALU.add).then_inc(conv_dve, 1)

            def bias_and_max(l, t):
                n = P * (t + 1)
                dve.wait_ge(pool_consts, 12)
                dve.wait_ge(scored, NB * l + t + 1)
                banks = ps[:, 0:4, :] if t else ps[:, 6:8, :]
                raw_s = banks.rearrange("p a (h s) -> p (a h) s", s=n)
                for h in range(NH):
                    dve.scalar_tensor_tensor(out=scores[t][:, h, 0:n], in0=ndist[:, 2 * P - n:2 * P], scalar=2.0 ** (-8.0 * (h + 1) / NH),
                                             in1=raw_s[:, head_place(h), :], op0=ALU.mult, op1=ALU.add).then_inc(biased, 1)
                dve.tensor_copy(scores[t][:, :, n], sink_b[:, l, :]).then_inc(biased, 1)
                dve.wait_ge(biased, (NH + 1) * (NB * l + t + 1))
                link(dve.tensor_reduce(mx[:, t, :], scores[t], AX.X, ALU.max))
                dve.tensor_scalar(mx[:, t, :], mx[:, t, :], -1.0, None, ALU.mult).then_inc(max_done, 1)

            def normalise(l, t):
                n = P * (t + 1)
                dve.wait_ge(exp_done, NH * (NB * l + t + 1))
                link(dve.reciprocal(pinv[:, t, :], psums[:, t, :]))
                dve.tensor_tensor(scores[t][:, :, 0:n], scores[t][:, :, 0:n],
                                  pinv[:, t, :].unsqueeze(2).to_broadcast([P, NH, n]), ALU.mult).then_inc(probs_done, 1)

            def front(l):
                b = S_FRONT[l]
                if l == 0:
                    norm(0, (0, 1))
                    low(2)
                else:
                    norm(2, (b + 2,))
                for j in range(3, 6):
                    low(b + j)
                dve.wait_ge(sig_done, l + 1)
                dve.tensor_tensor(hpad[:, :, PAD:PAD + S], ps[:, 4:6, :].rearrange("p a (c t) -> p (a c) t", c=2), sig, ALU.mult).then_inc(glu_done, 1)
                dve.wait_ge(glu_done, l + 1)
                low(b + 6)
                if l == 0:
                    dve.wait_ge(prm_turned, 1)
                    dve.tensor_copy(pcol[:, :, :, :].rearrange("p l c n -> p (l c n)"), ps[:, 3, 0:HEAD_COLS]).then_inc(prm_ready, 1)
                    dve.tensor_scalar(qkg[:, 0, :], ps[:, 3, HEAD_COLS:HEAD_COLS + L], HD ** -0.5, None, ALU.mult).then_inc(prm_ready, 1)
                    dve.tensor_copy(qkg[:, 1, :], ps[:, 3, HEAD_COLS + L:HEAD_COLS + 2 * L]).then_inc(prm_ready, 1)
                    dve.wait_ge(prm_ready, 3)
                else:
                    dve.wait_ge(zeros_stored, 16 * MAX_OVER)
                conv(l, 0, 5)
                dve.wait_ge(qk_sq_done, 2 * l + 1)
                dve.tensor_reduce(qkss[:, 0:NB * NH], q_sq.rearrange("p b (h d) -> p (b h) d", d=HD), AX.X, ALU.add).then_inc(qk_ss_done, 1)
                conv(l, 5, 7)
                dve.wait_ge(qk_sq_done, 2 * l + 2)
                dve.tensor_reduce(qkss[:, NB * NH:], k_sq.rearrange("p b (h d) -> p (b h) d", d=HD), AX.X, ALU.add).then_inc(qk_ss_done, 1)
                dve.wait_ge(qk_rms_done, l + 1)
                link(dve.reciprocal(qkr[:, :], qkr[:, :]))
                kr = qkr[:, NB * NH:].rearrange("p (b g) -> p b g", b=NB).unsqueeze(3).to_broadcast([P, NB, NKV, HD])
                k_ps = ps[:, 2, :].rearrange("p (b m d) -> p b m d", b=NB, d=HD)[:, :, 0:NKV, :]
                for r in range(2):
                    dve.tensor_tensor(kdup[:, :, :, r, :], k_ps, kr, ALU.mult).then_inc(qk_ready, 1)
                q3 = q_n.rearrange("p b (h d) -> p (b h) d", d=HD)
                dve.tensor_tensor(q3, ps[:, 0:2, :].rearrange("p b (h d) -> p (b h) d", d=HD),
                                  qkr[:, 0:NB * NH].unsqueeze(2).to_broadcast([P, NB * NH, HD]), ALU.mult).then_inc(qk_ready, 1)
                conv(l, 7, 13)
                low(b + 7)
                conv(l, 13, 16)
                bias_and_max(l, 0)
                conv(l, 16, 20)
                normalise(l, 0)
                bias_and_max(l, 1)
                conv(l, 20, 24)
                normalise(l, 1)
                conv(l, 24, TAPS)
                for t in range(NB):
                    dve.wait_ge(cat_high_done, 4 * l + t + 1)
                    dve.tensor_tensor(cat[1][:, 0:HP, t * P:(t + 1) * P], ps[:, 6 + t, :].rearrange("p (j q) -> p j q", j=HP),
                                      cat[0][:, 0:HP, t * P:(t + 1) * P], ALU.subtract).then_inc(cat_low_done, 1)
                low(b + 8)
                dve.wait_ge(ln_sum, 2 * l + 1)
                dve.tensor_tensor(cacc[:, :, :], cacc[:, :, :], ps[:, 0, 0:S].unsqueeze(1).to_broadcast([P, CC, S]), ALU.subtract).then_inc(ln_step, 1)
                low(b + 9)
                dve.wait_ge(ln_sd_done, l + 1)
                link(dve.reciprocal(ln_r, ln_sd))
                dve.tensor_tensor(cacc[:, :, :], cacc[:, :, :], ln_r.unsqueeze(1).to_broadcast([P, CC, S]), ALU.mult).then_inc(ln_step, 1)
                low(b + 10)
                for c in range(0, CC, 2):
                    dve.wait_ge(cat_high_done, 4 * l + 3 + c // 2)
                    dve.tensor_tensor(cat[1][:, CC + c:CC + c + 2, :], cacc[:, c:c + 2, :], cat[0][:, CC + c:CC + c + 2, :], ALU.subtract).then_inc(cat_low_done, 1)

            def route():
                dve.wait_ge(routed, 1)
                link(dve.tensor_copy(lg[:, :, :], ps[:, 4, 0:NB * NE].rearrange("p (b e) -> p b e", b=NB)))
                mine = lg[:, :, :].unsqueeze(3).to_broadcast([P, NB, NE, NE])
                other = lg[:, :, :].unsqueeze(2).to_broadcast([P, NB, NE, NE])
                dve.tensor_tensor(cmp_a[:, :, :, :], other, mine, ALU.is_gt)
                link(dve.tensor_tensor(cmp_b[:, :, :, :], other, mine, ALU.is_equal))
                link(dve.tensor_tensor(cmp_b[:, :, :, :], cmp_b[:, :, :, :], tri8[:, :, :].unsqueeze(1).to_broadcast([P, NB, NE, NE]), ALU.mult))
                link(dve.tensor_tensor(cmp_a[:, :, :, :], cmp_a[:, :, :, :], cmp_b[:, :, :, :], ALU.add))
                link(dve.tensor_reduce(rank[:, :, :], cmp_a[:, :, :, :], AX.X, ALU.add))
                link(dve.tensor_scalar(sel[:, :, :], rank[:, :, :], 2.0, None, ALU.is_lt))
                dve.sem_inc(sel_done, 1)
                for r in range(2):
                    link(dve.tensor_scalar(selr[:, r], rank[:, :, :], float(r), None, ALU.is_equal))
                for r in range(2):
                    link(dve.tensor_tensor(tmp8[:, r], selr[:, r], lg[:, :, :], ALU.mult))
                link(dve.tensor_reduce(top_l[:, :, :], tmp8[:, :, :, :], AX.X, ALU.add))
                dve.tensor_tensor(zt[:, :], top_l[:, 1], top_l[:, 0], ALU.subtract).then_inc(zdiff_done, 1)
                dve.wait_ge(counted, 1)
                link(dve.tensor_copy(pos[:, :, :], ps[:, 5, 0:NB * NE].rearrange("p (b e) -> p b e", b=NB)))
                link(dve.scalar_tensor_tensor(out=possel[:, :, :], in0=pos[:, :, :], scalar=1.0, in1=sel[:, :, :], op0=ALU.add, op1=ALU.mult))
                link(dve.tensor_scalar(possel[:, :, :], possel[:, :, :], -1.0, None, ALU.add))
                for e0, e1 in ((0, 1), (1, NE)):
                    for b in range(NB):
                        dve.tensor_tensor(onehot[:, b, e0:e1], iota_c[:, :].unsqueeze(1).to_broadcast([P, e1 - e0, P]),
                                          possel[:, b, e0:e1].unsqueeze(2).to_broadcast([P, e1 - e0, P]), ALU.is_equal).then_inc(onehot_done, 1)

            def place():
                link(dve.tensor_scalar(over_f[:, :], ps[:, 5, NB * NE:(NB + 1) * NE], float(P), None, ALU.is_gt))
                link(dve.tensor_copy(over_i[:, :], over_f[:, :]))
                link(dve.tensor_tensor(cmp_a[:, 0], tri8[:, :, :], over_f[:, :].unsqueeze(1).to_broadcast([P, NE, NE]), ALU.mult))
                link(dve.tensor_reduce(before_f[:, 0:NE], cmp_a[:, 0], AX.X, ALU.add))
                link(dve.tensor_reduce(before_f[:, NE:NE + 1], over_f[:, :], AX.X, ALU.add))
                dve.tensor_copy(before_i[:, :], before_f[:, :]).then_inc(over_ready, 1)
                link(dve.tensor_scalar(row_d[:, :], before_f[:, 0:NE], float(P), float(P * (NE - 1)), ALU.mult, ALU.add))
                link(dve.tensor_tensor(row_d[:, :], row_d[:, :], base_e[:, :], ALU.subtract))
                for b in range(NB):
                    link(dve.scalar_tensor_tensor(out=rank[:, b], in0=pos[:, b], scalar=float(P), in1=row_d[:, :], op0=ALU.is_ge, op1=ALU.mult))
                    link(dve.tensor_tensor(pos[:, b], pos[:, b], rank[:, b], ALU.add))
                    link(dve.tensor_tensor(pos[:, b], pos[:, b], base_e[:, :], ALU.add))
                for r in range(2):
                    link(dve.tensor_tensor(tmp8[:, r], selr[:, r], pos[:, :, :], ALU.mult))
                link(dve.tensor_reduce(row_f[:, :, :], tmp8[:, :, :, :], AX.X, ALU.add))
                dve.tensor_copy(row_i[:, :, :], row_f[:, :, :]).then_inc(rows_ready, 1)
                dve.wait_ge(z_done, 1)
                link(dve.tensor_scalar(den[:, :], zt[:, :], 1.0, None, ALU.add))
                link(dve.reciprocal(top_w[:, 0], den[:, :]))
                link(dve.tensor_tensor(top_w[:, 1], zt[:, :], top_w[:, 0], ALU.mult))

            def gather_low(i, per, e):
                for j in range(2):
                    dve.wait_ge(xg_high_done, at(i, 2 * per, 2 * e + j + 1))
                    dst = xg[1][:, 4 * j:4 * j + 4, e % 2, :]
                    dve.tensor_tensor(dst, ps[:, (3, 6)[j], :].rearrange("p (k c) -> p k c", k=4),
                                      xg[0][:, 4 * j:4 * j + 4, e % 2, :], ALU.subtract).then_inc(xg_low_done, 1)

            def expert_steps(s, n, e, experts, following, i, pers):
                per_s, per_n, per_e = pers
                for k in range(experts * EG):
                    last = k == experts * EG - 1 and not following
                    t = s + 6 * k
                    if not last:
                        low(t + 2, i, per_s)
                    dve.wait_ge(act_high_done, at(i, per_n, DG + n + k + 1))
                    dve.tensor_tensor(act_part[1][:, k % 2, :], ps[:, 2, :], act_part[0][:, k % 2, :], ALU.subtract).then_inc(act_low_done, 1)
                    if last:
                        continue
                    low(t + 3, i, per_s)
                    low(t + 4, i, per_s)
                    low(t + 5, i, per_s)
                    if k % EG == GATHER_AT and (k // EG + 1 < experts or following):
                        gather_low(i, per_e, e + k // EG + 1)
                    dve.wait_ge(w_used, at(i, per_s, t + 4))
                    dve.wait_ge(silu_done, at(i, per_n, DG + n + k + 2))
                    dve.tensor_tensor(prod_t, ps[:, 1, :], silu_t, ALU.mult).then_inc(prod_done, 1)
                    low(t + 6, i, per_s)
                    low(t + 7, i, per_s)

            dve.memset(eps_t[:, :], EPS).then_inc(dve_consts, 1)
            dve.memset(ones[:, :], 1.0).then_inc(dve_consts, 1)
            dve.memset(mean_w[:, :], 1.0 / CW).then_inc(dve_consts, 1)
            dve.memset(hpad[:, :, 0:PAD], 0.0).then_inc(dve_consts, 1)
            dve.memset(zero_r[:, :].bitcast(F32), 0.0).then_inc(dve_consts, 1)
            front(0)
            b = S_DENSE
            low(b)
            norm(1, (b + 1, b + 2))
            low(b + 3)
            dve.wait_ge(w_used, b + 2)
            dve.wait_ge(silu_done, 1)
            dve.tensor_tensor(prod_t, ps[:, 1, :], silu_t, ALU.mult).then_inc(prod_done, 1)
            dve.wait_ge(act_high_done, 1)
            dve.tensor_tensor(act_part[1][:, 0, :], prod_t, act_part[0][:, 0, :], ALU.subtract).then_inc(act_low_done, 1)
            low(b + 4)
            with dve.Fori(0, (DG - 1) // 2) as i:
                for u in range(2):
                    t = b + 2 + 3 * u
                    low(t + 3, i, 6)
                    dve.wait_ge(w_used, at(i, 6, t + 2))
                    dve.wait_ge(silu_done, at(i, 2, u + 2))
                    dve.wait_ge(act_low_done, at(i, 2, u + 1))
                    dve.tensor_tensor(prod_t, ps[:, 2 * (1 - u) + 1, :], silu_t, ALU.mult).then_inc(prod_done, 1)
                    low(t + 4, i, 6)
                    dve.wait_ge(act_high_done, at(i, 2, u + 2))
                    dve.tensor_tensor(act_part[1][:, 1 - u, :], prod_t, act_part[0][:, 1 - u, :], ALU.subtract).then_inc(act_low_done, 1)
                    low(t + 5, i, 6)
            front(1)
            low(S_MOE)
            norm(3, (S_MOE + 1,), split=False)
            route()
            low(S_MOE + 2)
            gather_low(None, 0, 0)
            low(S_MOE + 3)
            place()
            n_passes = passes_in_all(dve)
            dve.wait_ge(w_used, S_MOE + 4)
            dve.wait_ge(silu_done, DG + 1)
            dve.tensor_tensor(prod_t, ps[:, 1, :], silu_t, ALU.mult).then_inc(prod_done, 1)
            low(S_MOE + 4)
            low(S_MOE + 5)
            with dve.Fori(0, NE // 2 - 1) as i:
                expert_steps(S_MOE + 4, 0, 0, 2, True, i, (PAIR, 2 * EG, 2))
            expert_steps(S_MOE + 4 + (NE // 2 - 1) * PAIR, (NE - 2) * EG, NE - 2, 2, False, None, (0, 0, 0))

            def one_pass(e, m):
                dve.tensor_scalar(pos[:, :, :], possel[:, :, :], -float(P), None, ALU.add).then_inc(shifted, 1)
                dve.wait_ge(shifted, m + 1)
                for b in range(NB):
                    dve.tensor_tensor(onehot[:, b], iota_c[:, :].unsqueeze(1).to_broadcast([P, NE, P]),
                                      pos[:, b, :].unsqueeze(2).to_broadcast([P, NE, P]), ALU.is_equal).then_inc(onehot_done, 1)
                for j in range(3):
                    low(S_OVER + j, m, OVER)
                gather_low(m, 1, NE)
                low(S_OVER + 3, m, OVER)
                low(S_OVER + 4, m, OVER)
                dve.wait_ge(w_used, at(m, OVER, S_OVER + 4))
                dve.wait_ge(silu_done, at(m, EG, DG + NE * EG + 1))
                dve.tensor_tensor(prod_t, ps[:, 1, :], silu_t, ALU.mult).then_inc(prod_done, 1)
                low(S_OVER + 5, m, OVER)
                expert_steps(S_OVER + 4, NE * EG, NE, 1, False, m, (OVER, EG, 1))

            overflow_passes(dve, n_passes, one_pass)
            for b in range(NB):
                for r in range(2):
                    dve.wait_ge(rows_fetched[2 * r + b], 16)
                    if r:
                        dve.wait_ge(combined, 2 * b + 1)
                    dve.scalar_tensor_tensor(out=xr[:, b, :], in0=y_rows[:, 2 * r + b, :], scalar=top_w[:, r, b:b + 1],
                                             in1=xr[:, b, :], op0=ALU.mult, op1=ALU.add).then_inc(combined, 1)

        @block.tensor
        def _(pe):
            def mm(out_, lhsT, rhs, start, stop=False):
                return pe.matmul(out_, lhsT, rhs, start=start, stop=stop, skip_group_check=True)

            def terms(out_, tokens, tidx, weights, widx, start, stop, weights_move=True):
                for n, (a, w) in enumerate(TERMS):
                    x_ = tokens[a][tidx]
                    w_ = weights[w][widx]
                    lhsT, rhs = (x_, w_) if weights_move else (w_, x_)
                    last = mm(out_, lhsT, rhs, start and n == 0, stop and n == 2)
                return last

            def slot(s, k, i=None, per=0):
                pe.wait_ge(w_low_done, at(i, per, s + 1))
                return [part_slot(0, s, k), part_slot(1, s, k)]

            def order(last_slot):
                return [(0, 0), (0, 1), (1, 0), (1, 1)] if last_slot else [(0, 0), (1, 0), (0, 1), (1, 1)]

            def norm_turn(q):
                for b in range(NB):
                    pe.wait_ge(h_done, 2 * q + b + 1)
                    for k in range(KC):
                        last = pe.transpose(ps[:, k // 2, (k % 2) * S + b * P:(k % 2) * S + (b + 1) * P],
                                            h_td[:, b, k * P:(k + 1) * P], ident[:, :])
                        if b == 1 and k % 2:
                            last.then_inc(h_turned, 1)

            def front(l):
                b = S_FRONT[l]
                norm_turn(2 * l)
                for m in range(2):
                    for j in range(2):
                        w = slot(b + 2 * m + j, 4)
                        if m == 0:
                            pe.wait_ge(hT_low_done, 8 * l + 2 * j + 2)
                        for c in range(CC):
                            o = ps[:, 4 + 2 * m + c // 2, (c % 2) * S:(c % 2 + 1) * S]
                            for k in range(4):
                                last = terms(o, hT, (slice(None), 4 * j + k, slice(None)), w, (slice(None), k, slice(c * P, (c + 1) * P)),
                                             j == 0 and k == 0 and c % 2 == 0, j == 1 and k == 3, weights_move=False)
                        last.then_inc(w_used, 1)
                if l == 0:
                    pe.wait_ge(consts_loaded, CONST_LOADS)
                    for m in range(L):
                        for c in range(CC):
                            o = (m * CC + c) * NPRM
                            pe.transpose(ps[:, 3, o:o + NPRM], prm[:, m, c * P:(c + 1) * P], ident[0:NPRM, 0:NPRM])
                    pe.transpose(ps[:, 3, HEAD_COLS:HEAD_COLS + 2 * L], head_rows, ident[0:2 * L, 0:2 * L]).then_inc(prm_turned, 1)
                for j in range(2):
                    w = slot(b + 4 + j, 4)
                    for k in range(4):
                        for t in range(NB):
                            last = terms(ps[:, t, :], hT, (slice(None), 4 * j + k, slice(t * P, (t + 1) * P)), w, (slice(None), k, slice(None)),
                                         j == 0 and k == 0, j == 1 and k == 3)
                    last.then_inc(w_used, 1)
                w = slot(b + 6, 8)
                for k in range(8):
                    for t in range(NB):
                        last = terms(ps[:, 2, t * 2 * KVW:(t + 1) * 2 * KVW], hT, (slice(None), k, slice(t * P, (t + 1) * P)), w, (slice(None), k, slice(None)),
                                     k == 0 and t == 0, k == 7)
                last.then_inc(w_used, 1)
                if l == 0:
                    pe.wait_ge(prm_ready, 3)
                pe.wait_ge(qk_ready, 3 * l + 2)
                for t in range(NB):
                    for g in range(NKV):
                        last = pe.transpose(ps[:, 3, g * S + t * P:g * S + (t + 1) * P], kdup[:, t, g].rearrange("p r d -> p (r d)"), ident[:, :])
                last.then_inc(qk_turned, 1)
                pe.wait_ge(qk_ready, 3 * l + 3)
                pe.wait_ge(glu_done, l + 1)
                for t in range(NB):
                    for j in range(HP):
                        last = pe.transpose(ps[:, 4 + j // 2, (j % 2) * S + t * P:(j % 2) * S + (t + 1) * P], q_n[:, t, j * P:(j + 1) * P], ident[:, :])
                last.then_inc(qk_turned, 1)
                pe.wait_ge(qkT_done, 2 * l + 2)
                pe.wait_ge(v_done, l + 1)
                for t in range(NB):
                    n = P * (t + 1)
                    per_bank = 512 // n
                    for h in range(NH):
                        r, m = h % 2, head_place(h)
                        o = ps[:, (0 if t else 6) + m // per_bank, (m % per_bank) * n:(m % per_bank + 1) * n]
                        last = mm(o, qT[r * HD:(r + 1) * HD, h // 2, t * P:(t + 1) * P], kT[r * HD:(r + 1) * HD, h // (NH // NKV), 0:n], True, True)
                    last.then_inc(scored, 1)
                for m, (t, kb, bank) in enumerate(((0, 0, 4), (1, 0, 0), (1, 1, 2))):
                    pe.wait_ge(probs_done, NB * l + t + 1)
                    for h in range(NH):
                        last = pe.transpose(ps[:, bank + h // 4, (h % 4) * P:(h % 4 + 1) * P], scores[t][:, h, kb * P:(kb + 1) * P], ident[:, :])
                    last.then_inc(p_turned, 1)
                    if m == 1:
                        continue
                    pe.wait_ge(pT_done, 3 * l + (1, 3)[t])
                    for g in range(NKV):
                        for r in range(2):
                            h0 = g * (NH // NKV) + r
                            o = ps[r * HD:(r + 1) * HD, 6 + t, 2 * g * P:(2 * g + 2) * P]
                            for kb in range(t + 1):
                                last = mm(o, v_sb[:, kb, g * HD:(g + 1) * HD], pT[:, t + kb, h0:h0 + 3:2, :], kb == 0, kb == t)
                    last.then_inc(pv_done, 1)
                def project(j):
                    w = slot(b + 7 + j, 2)
                    for t, k in order(j == 3):
                        for hf in range(2):
                            last = terms(ps[:, 4 + 2 * t + hf, :], cat, (slice(None), 2 * j + k, slice(t * P, (t + 1) * P)), w, (slice(None), k, slice(hf * 512, (hf + 1) * 512)),
                                         j == 0 and k == 0, j == 3 and k == 1)
                        if j == 3 and (t, k) == (0, 1):
                            last.then_inc(block0_projected, 1)
                    last.then_inc(w_used, 1)
                pe.wait_ge(conv_dve, 2 * TAPS * (l + 1))
                pe.wait_ge(conv_pool, (TAPS - 1) * (l + 1))
                for c in range(CC):
                    last = mm(ps[:, 0, 0:S], mean_w[:, :], cacc[:, c, :], c == 0, c == CC - 1)
                last.then_inc(ln_sum, 1)
                pe.wait_ge(cat_low_done, 4 * l + 2)
                project(0)
                pe.wait_ge(ln_sq_done, l + 1)
                for c in range(CC):
                    last = mm(ps[:, 1, 0:S], mean_w[:, :], ln_sq[:, c, :], c == 0, c == CC - 1)
                last.then_inc(ln_sum, 1)
                project(1)
                pe.wait_ge(cat_low_done, 4 * l + 3)
                project(2)
                pe.wait_ge(cat_low_done, 4 * l + 4)
                project(3)

            def dense_gate_up(s, u, i=None):
                for m in range(2):
                    w = slot(s + m, 8, i, 6)
                    for f in range(2):
                        for k in range(KC):
                            last = terms(ps[:, 2 * u + m, f * S:(f + 1) * S], hT, (slice(None), k, slice(None)), w, (slice(None), k, slice(f * P, (f + 1) * P)),
                                         f == 0 and k == 0, k == KC - 1, weights_move=False)
                    last.then_inc(w_used, 1)

            def dense_down(s, u, start, stop, i=None):
                w = slot(s, 2, i, 6)
                a = [t[:, u, :].rearrange("p (f t) -> p f t", f=2) for t in act_part]
                for t, f in order(stop):
                    for hf in range(2):
                        last = terms(ps[:, 4 + 2 * t + hf, :], a, (slice(None), f, slice(t * P, (t + 1) * P)), w, (slice(None), f, slice(hf * 512, (hf + 1) * 512)),
                                     start and f == 0, stop and f == 1)
                    if stop and (t, f) == (0, 1):
                        last.then_inc(block0_projected, 1)
                last.then_inc(w_used, 1)

            def gather(i, per, e, e_reg):
                for j in range(2):
                    for k in range(4):
                        for b in range(NB):
                            last = mm(ps[:, (3, 6)[j], k * P:(k + 1) * P], h_td[:, b, (4 * j + k) * P:(4 * j + k + 1) * P],
                                      onehot[:, b, e_reg, :], k == 0 and b == 0, b == 1)
                    last.then_inc(gathered, 1)

            def gate_up(s, r, i, per):
                for m in range(2):
                    for j in range(2):
                        w = slot(s + 2 * m + j, 4, i, per)
                        for k in range(4):
                            last = terms(ps[:, m, :], xg, (slice(None), 4 * j + k, r, slice(None)), w, (slice(None), k, slice(None)),
                                         j == 0 and k == 0, j == 1 and k == 3)
                        last.then_inc(w_used, 1)

            def turn_act():
                for f in range(4):
                    last = pe.transpose(ps[:, 2, f * P:(f + 1) * P], prod_t[:, f * P:(f + 1) * P], ident[:, :])
                last.then_inc(act_turned, 1)

            def expert_steps(s, n, e, experts, following, i, pers, e_reg):
                per_s, per_n, per_e = pers
                for k in range(experts * EG):
                    last_step = k == experts * EG - 1 and not following
                    t = s + 6 * k
                    if not last_step:
                        pe.wait_ge(silu_done, at(i, per_n, DG + n + k + 1))
                        pe.wait_ge(prod_done, at(i, per_n, DG + n + k + 1))
                        nxt = (k + 1) // EG
                        if k % EG == EG - 1:
                            pe.wait_ge(xg_low_done, at(i, 2 * per_e, 2 * (e + nxt + 1)))
                        gate_up(t, (e + nxt) % 2, i, per_s)
                        if k % EG == GATHER_AT and (k // EG + 1 < experts or following):
                            gather(i, per_e, e + k // EG + 1, e_reg(k // EG + 1))
                    pe.wait_ge(act_low_done, at(i, per_n, DG + n + k + 1))
                    if k % EG == 0:
                        pe.wait_ge(y_copied, at(i, per_e, e + k // EG + 1))
                    for j in range(2):
                        w = slot(t + (0 if last_step else 4) + j, 2, i, per_s)
                        a = [p_[:, k % 2, :].rearrange("p (f c) -> p f c", f=4) for p_ in act_part]
                        for f in range(2):
                            for hf in range(2):
                                last = terms(ps[:, 4 + hf, :], a, (slice(None), 2 * j + f, slice(None)), w, (slice(None), f, slice(hf * 512, (hf + 1) * 512)),
                                             k % EG == 0 and j == 0 and f == 0, k % EG == EG - 1 and j == 1 and f == 1)
                        last.then_inc(w_used, 1)
                    if not last_step:
                        pe.wait_ge(prod_done, at(i, per_n, DG + n + k + 2))
                        turn_act()

            pe.wait_ge(ident_ready, 2)
            pe.wait_ge(dve_consts, DVE_CONSTS)
            front(0)
            b = S_DENSE
            norm_turn(1)
            pe.wait_ge(hT_low_done, 8)
            dense_gate_up(b, 0)
            for bank in range(4, 8):
                mm(ps[:, bank, 0:P], zero_r[:, :], zero_r[:, :], True)
            with pe.Fori(0, (DG - 1) // 2) as i:
                for u in range(2):
                    t = b + 2 + 3 * u
                    dense_gate_up(t, 1 - u, i)
                    pe.wait_ge(act_low_done, at(i, 2, u + 1))
                    dense_down(t + 2, u, False, False, i)
            pe.wait_ge(act_low_done, DG)
            dense_down(S_FRONT[1] - 1, 0, False, True)
            front(1)
            norm_turn(3)
            pe.wait_ge(hT_plain_done, 4)
            for t in range(NB):
                for k in range(KC):
                    last = mm(ps[:, 4, t * NE:(t + 1) * NE], hT_plain[:, k, t * P:(t + 1) * P], wr[:, k, :], k == 0 and t == 0, k == KC - 1)
            last.then_inc(routed, 1)
            pe.wait_ge(sel_done, 1)
            pe.wait_ge(pool_consts, 12)
            mm(ps[:, 5, 0:NE], tri[:, :], sel[:, 0, :], True, True)
            mm(ps[:, 5, NE:2 * NE], tri[:, :], sel[:, 1, :], False)
            mm(ps[:, 5, NE:2 * NE], ones[:, :], sel[:, 0, :], False, True)
            mm(ps[:, 5, 2 * NE:3 * NE], ones[:, :], sel[:, 0, :], False)
            mm(ps[:, 5, 2 * NE:3 * NE], ones[:, :], sel[:, 1, :], False, True).then_inc(counted, 1)
            pe.wait_ge(onehot_done, 2)
            gather(None, 0, 0, 0)
            pe.wait_ge(xg_low_done, 2)
            gate_up(S_MOE, 0, None, 0)
            pe.wait_ge(onehot_done, 4)
            n_passes = passes_in_all(pe)
            pe.wait_ge(prod_done, DG + 1)
            turn_act()
            with pe.Fori(0, NE // 2 - 1) as i:
                expert_steps(S_MOE + 4, 0, 0, 2, True, i, (PAIR, 2 * EG, 2), lambda k: i * 2 + k)
            expert_steps(S_MOE + 4 + (NE // 2 - 1) * PAIR, (NE - 2) * EG, NE - 2, 2, False, None, (0, 0, 0), lambda k: NE - 2 + k)

            def one_pass(e, m):
                pe.wait_ge(onehot_done, at(m, 2, 6))
                gather(m, 1, NE, e)
                pe.wait_ge(silu_done, at(m, EG, DG + NE * EG))
                pe.wait_ge(prod_done, at(m, EG, DG + NE * EG))
                pe.wait_ge(xg_low_done, at(m, 2, 2 * (NE + 1)))
                gate_up(S_OVER, 0, m, OVER)
                pe.wait_ge(prod_done, at(m, EG, DG + NE * EG + 1))
                turn_act()
                expert_steps(S_OVER + 4, NE * EG, NE, 1, False, m, (OVER, EG, 1), None)

            overflow_passes(pe, n_passes, one_pass)


_INS = ["x", "attn_norm_g", "w_in", "q_norm_g", "k_norm_g", "sinks", "conv_w", "conv_b", "conv_ln_g", "conv_ln_b", "w_out",
        "ffn_norm_g", "dense_w_gate", "dense_w_up", "dense_w_down", "w_router", "moe_w_gate", "moe_w_up", "moe_w_down"]


def kernel(**inputs):
    import numpy as np
    import concourse.bacc as bacc
    from concourse.bass_utils import run_bass_kernel_spmd

    nc = bacc.Bacc("TRN2", target_bir_lowering=False, num_devices=1)
    arrays, args = {}, []
    for name in _INS:
        a = np.ascontiguousarray(inputs[name])
        arrays[f"in_{name}"] = a
        args.append(nc.dram_tensor(f"in_{name}", a.shape, mybir.dt.from_np(a.dtype), kind="ExternalInput").ap())
    args.append(nc.dram_tensor("out", inputs["x"].shape, F32, kind="ExternalOutput").ap())
    hybrid_trunk(nc, *args)
    r = run_bass_kernel_spmd(nc, [arrays], core_ids=[0])
    return r.results[0]["out"]
```
